# Optimizing a Trainium2 kernel written in Bass

```python
import math
import jax, jax.numpy as jnp
from jax import lax
import numpy as np

D_MODEL = 1024
BATCH = 1
SEQ = 256
DEPTH = 2

GRID_W = 64
CTX_LEN = 256
N_MIXERS = 3
N_MOD = 9
D_FF = 2816
MACARON_W = 0.5
NORM_EPS = 1e-6
NEG_INF = -1e9

DA_HEADS = 8
DA_HEAD_DIM = 64
DA_Q_BLOCK = 128
ROPE_BASE = 10000.0
ROPE_PAIRS = DA_HEAD_DIM // 4

NA_HEADS = 16
NA_HEAD_DIM = D_MODEL // NA_HEADS
NA_ROWS = 8
NA_COLS = 16

RW_HEAD = 64
RW_HEADS = D_MODEL // RW_HEAD
RW_DECAY_LORA = 64
RW_AAA_LORA = 64
RW_GATE_LORA = 160
RW_LN_EPS = 64e-5


def _rmsnorm(h, g):
    hf = h.astype(jnp.float32)
    hf = hf * lax.rsqrt(jnp.mean(hf * hf, axis=-1, keepdims=True) + NORM_EPS)
    return hf.astype(h.dtype) * g

def _modulate(h, shift, scale):
    return h * (1 + scale) + shift

def _ffn_sublayer(h, mod, g_pre, g_post, w_in, w_out):
    shift, scale, gate = mod
    u = _modulate(_rmsnorm(h, g_pre), shift, scale)
    a, b = jnp.split(u @ w_in, 2, axis=-1)
    y = (jax.nn.silu(a) * b) @ w_out
    return h + MACARON_W * gate * _rmsnorm(y, g_post)

def _axial_rope_tables(seq_len):
    t = jnp.arange(seq_len)
    pos = jnp.stack([t // GRID_W, t % GRID_W], axis=-1).astype(jnp.float32)
    freq = ROPE_BASE ** (-jnp.arange(ROPE_PAIRS, dtype=jnp.float32) / ROPE_PAIRS)
    ang = pos[:, :, None] * freq
    return jnp.cos(ang), jnp.sin(ang)

def _axial_rope(x, cos, sin):
    d = x.shape[-1]
    xr = x.reshape(x.shape[:-1] + (2, 2, d // 4))
    x1, x2 = xr[..., 0, :], xr[..., 1, :]
    bshape = (cos.shape[0],) + (1,) * (x.ndim - 3) + (2, d // 4)
    c = cos.reshape(bshape).astype(x.dtype)
    s = sin.reshape(bshape).astype(x.dtype)
    return jnp.stack([x1 * c - x2 * s, x2 * c + x1 * s], axis=-2).reshape(x.shape)

def _attend(q, k, v):
    s = jnp.einsum('bthd,bkhd->bhtk', q, k).astype(jnp.float32)
    p = jax.nn.softmax(s, axis=-1).astype(v.dtype)
    return jnp.einsum('bhtk,bkhd->bthd', p, v)

def _diff_attend(q, k, v, lam):
    s = jnp.einsum('bthjd,bkhjd->bhjtk', q, k).astype(jnp.float32)
    p = jax.nn.softmax(s, axis=-1)
    p = p[:, :, 0] - lam.astype(jnp.float32) * p[:, :, 1]
    return jnp.einsum('bhtk,bkhe->bthe', p.astype(v.dtype), v)

def _diff_attention(uc, ux, w_in, w_out, lam_vec, subln_g, lam_init, cos, sin, need_ctx):
    B, S, D = ux.shape
    H, d = DA_HEADS, DA_HEAD_DIM

    def proj(u):
        L = u.shape[1]
        q, k, v = jnp.split(u @ w_in, 3, axis=-1)
        return (q.reshape(B, L, H, 2, d) * d ** -0.5, k.reshape(B, L, H, 2, d), v.reshape(B, L, H, 2 * d))

    qc, kc, vc = proj(uc)
    qx, kx, vx = proj(ux)
    qx = _axial_rope(qx, cos, sin)
    kx = _axial_rope(kx, cos, sin)
    lam = (jnp.exp(jnp.sum(lam_vec[0] * lam_vec[1])) - jnp.exp(jnp.sum(lam_vec[2] * lam_vec[3]))
           + lam_init)
    k_all = jnp.concatenate([kc, kx], axis=1)
    v_all = jnp.concatenate([vc, vx], axis=1)
    nb = S // DA_Q_BLOCK
    qb = jnp.moveaxis(qx.reshape(B, nb, DA_Q_BLOCK, H, 2, d), 1, 0)
    ox = lax.map(lambda q: _diff_attend(q, k_all, v_all, lam), qb)
    ox = jnp.moveaxis(ox, 0, 1).reshape(B, S, H, 2 * d)

    def out(o):
        o = _rmsnorm(o, subln_g) * (1 - lam_init)
        return o.reshape(o.shape[0], o.shape[1], H * 2 * d) @ w_out

    yx = out(ox)
    yc = out(_diff_attend(qc, kc, vc, lam)) if need_ctx else None
    return yc, yx

def _neighbourhood_attention(uc, ux, w_in, w_out, rpb, need_ctx):
    B, S, D = ux.shape
    C = uc.shape[1]
    H, d = NA_HEADS, NA_HEAD_DIM
    rows = S // GRID_W
    kr = min(NA_ROWS, rows)

    def proj(u):
        L = u.shape[1]
        q, k, v = jnp.split(u @ w_in, 3, axis=-1)
        return q.reshape(B, L, H, d) * d ** -0.5, k.reshape(B, L, H, d), v.reshape(B, L, H, d)

    qc, kc, vc = proj(uc)
    qx, kx, vx = proj(ux)
    q_grid = qx.reshape(B, rows, GRID_W, H, d)
    k_grid = kx.reshape(B, rows, GRID_W, H, d)
    v_grid = vx.reshape(B, rows, GRID_W, H, d)
    col = jnp.arange(GRID_W)
    col_start = jnp.clip(col - NA_COLS // 2, 0, GRID_W - NA_COLS)
    col_in = (col[None, :] >= col_start[:, None]) & (col[None, :] < col_start[:, None] + NA_COLS)
    col_off = jnp.clip(col[None, :] - col[:, None] + NA_COLS - 1, 0, 2 * NA_COLS - 2)
    col_bias = jnp.where(col_in, rpb[:, :, col_off].astype(jnp.float32), NEG_INF)

    def row_block(r):
        rs = jnp.clip(r - kr // 2, 0, rows - kr)
        q = lax.dynamic_index_in_dim(q_grid, r, axis=1, keepdims=False)
        kb = lax.dynamic_slice_in_dim(k_grid, rs, kr, axis=1)
        vb = lax.dynamic_slice_in_dim(v_grid, rs, kr, axis=1)
        bias = jnp.swapaxes(col_bias[:, rs + jnp.arange(kr) - r + NA_ROWS - 1], 1, 2)
        s_lat = jnp.einsum('bqhd,brkhd->bhqrk', q, kb).astype(jnp.float32) + bias
        s_ctx = jnp.einsum('bqhd,bchd->bhqc', q, kc).astype(jnp.float32)
        s = jnp.concatenate([s_ctx, s_lat.reshape(B, H, GRID_W, kr * GRID_W)], axis=-1)
        p = jax.nn.softmax(s, axis=-1).astype(vx.dtype)
        p_ctx = p[..., :C]
        p_lat = p[..., C:].reshape(B, H, GRID_W, kr, GRID_W)
        return (jnp.einsum('bhqc,bchd->bqhd', p_ctx, vc)
                + jnp.einsum('bhqrk,brkhd->bqhd', p_lat, vb))

    ox = lax.map(row_block, jnp.arange(rows))
    yx = jnp.moveaxis(ox, 0, 1).reshape(B, S, D) @ w_out
    yc = _attend(qc, kc, vc).reshape(B, C, D) @ w_out if need_ctx else None
    return yc, yx

def _rwkv7_prep(u, mu, w_in, w0, w1, w2, a0, a1, a2, g1, g2, k_k, k_a):
    B, L, D = u.shape
    H, N = RW_HEADS, RW_HEAD
    f32 = jnp.float32
    zero = jnp.zeros_like(u[:, :1])
    xx = 0.5 * (jnp.concatenate([zero, u[:, :-1]], axis=1) + jnp.concatenate([u[:, 1:], zero], axis=1)) - u
    xr, xw, xk, xv, xa, xg = [u + xx * mu[j] for j in range(6)]
    w_r, w_k, w_v = jnp.split(w_in, 3, axis=1)
    r = xr @ w_r
    k = xk @ w_k
    v = xv @ w_v
    lora_w = jnp.einsum('zblr,zrd->zbld', jnp.tanh(jnp.einsum('bld,zdr->zblr', xw, w1)), w2)
    w_log = -jax.nn.softplus(-(w0[:, None, None, :] + lora_w).astype(f32)) - 0.5
    decay = jnp.exp(-jnp.exp(w_log))
    a = jax.nn.sigmoid(a0[:, None, None, :]
                       + jnp.einsum('zblr,zrd->zbld', jnp.einsum('bld,zdr->zblr', xa, a1), a2))
    g = jax.nn.sigmoid(xg @ g1) @ g2
    kk = (k * k_k).reshape(B, L, H, N).astype(f32)
    kk = kk / jnp.maximum(jnp.linalg.norm(kk, axis=-1, keepdims=True), 1e-12)
    kd = k[None] * (1 + (a - 1) * k_a)

    def heads(t):
        return t.reshape(t.shape[:-1] + (H, N)).astype(f32)

    def two(t):
        return jnp.broadcast_to(t, (2,) + t.shape)

    def orient(t):
        t = jnp.stack([t[0], jnp.flip(t[1], axis=1)])
        return jnp.moveaxis(t, 2, 0)

    scan_in = (orient(two(heads(r))), orient(heads(decay)), orient(heads(kd)),
               orient(two(heads(v))), orient(two(-kk)), orient(kk[None] * heads(a)))
    return scan_in, (r, kd, v, g)

def _wkv7_scan(state0, r, w, k, v, a, b):
    def step(S, inp):
        rt, wt, kt, vt, at, bt = inp
        sa = jnp.einsum('zbhvk,zbhk->zbhv', S, at)
        S = S * wt[..., None, :] + sa[..., :, None] * bt[..., None, :] + vt[..., :, None] * kt[..., None, :]
        return S, jnp.einsum('zbhvk,zbhk->zbhv', S, rt)
    return lax.scan(step, state0, (r, w, k, v, a, b))

def _rwkv7_readout(y, r, kd, v, g, r_k, ln_g, ln_b, w_out):
    B, L, D = r.shape
    H, N = RW_HEADS, RW_HEAD
    y = jnp.moveaxis(y, 0, 2)
    y = y[0] + jnp.flip(y[1], axis=1)
    mean = jnp.mean(y, axis=-1, keepdims=True)
    var = jnp.mean(jnp.square(y - mean), axis=-1, keepdims=True)
    y = ((y - mean) * lax.rsqrt(var + RW_LN_EPS)).reshape(B, L, D).astype(r.dtype) * ln_g + ln_b
    rh = r.reshape(B, L, H, N)
    kh = (kd[0] + kd[1]).reshape(B, L, H, N)
    bonus = jnp.sum(rh * kh * r_k, axis=-1, keepdims=True) * v.reshape(B, L, H, N)
    return ((y + bonus.reshape(B, L, D)) * g) @ w_out

def _rwkv7_mixer(uc, ux, mu, w_in, w_out, w0, w1, w2, a0, a1, a2, g1, g2, k_k, k_a, r_k,
                 ln_g, ln_b, need_ctx):
    B = ux.shape[0]
    in_c, aux_c = _rwkv7_prep(uc, mu, w_in, w0, w1, w2, a0, a1, a2, g1, g2, k_k, k_a)
    in_x, aux_x = _rwkv7_prep(ux, mu, w_in, w0, w1, w2, a0, a1, a2, g1, g2, k_k, k_a)
    s0 = jnp.zeros((2, B, RW_HEADS, RW_HEAD, RW_HEAD), jnp.float32)
    s_ctx, y_c = _wkv7_scan(s0, *in_c)
    _, y_x = _wkv7_scan(s_ctx, *in_x)
    yx = _rwkv7_readout(y_x, *aux_x, r_k, ln_g, ln_b, w_out)
    yc = _rwkv7_readout(y_c, *aux_c, r_k, ln_g, ln_b, w_out) if need_ctx else None
    return yc, yx

def first_inputs(seed: int = 0) -> dict:
    key = jax.random.key(seed)
    ks = iter(jax.random.split(key, 48))
    f32 = jnp.float32
    D, F = D_MODEL, D_FF
    n_a, n_b, n_c = [len(range(m, DEPTH, N_MIXERS)) for m in range(N_MIXERS)]

    def nrm(shape, scale):
        return jax.random.normal(next(ks), shape, f32) * scale

    def gain(shape):
        return 1.0 + nrm(shape, 0.05)

    return {
        'x': nrm((BATCH, SEQ, D), 1.0),
        'c': nrm((BATCH, D), 1.0),
        'ctx': nrm((BATCH, CTX_LEN, D), 1.0),
        'c_ctx': nrm((D,), 1.0),
        'ada_w': nrm((DEPTH, D, N_MOD * D), 0.5 * D ** -0.5),
        'ada_b': nrm((DEPTH, N_MOD * D), 0.02),
        'norm_g': gain((DEPTH, 6, D)),
        'ffn_w_in': nrm((DEPTH, 2, D, 2 * F), D ** -0.5),
        'ffn_w_out': nrm((DEPTH, 2, F, D), F ** -0.5),
        'da_w_in': nrm((n_a, D, 3 * D), D ** -0.5),
        'da_w_out': nrm((n_a, D, D), D ** -0.5),
        'da_lambda': nrm((n_a, 4, DA_HEAD_DIM), 0.1),
        'da_subln_g': gain((n_a, 2 * DA_HEAD_DIM)),
        'na_w_in': nrm((n_b, D, 3 * D), D ** -0.5),
        'na_w_out': nrm((n_b, D, D), D ** -0.5),
        'na_rpb': nrm((n_b, NA_HEADS, 2 * NA_ROWS - 1, 2 * NA_COLS - 1), 0.2),
        'rw_mu': jax.random.uniform(next(ks), (n_c, 6, D), f32),
        'rw_w_in': nrm((n_c, D, 3 * D), D ** -0.5),
        'rw_w_out': nrm((n_c, D, D), D ** -0.5),
        'rw_w0': jax.random.uniform(next(ks), (n_c, 2, D), f32, -6.0, -1.0),
        'rw_w1': nrm((n_c, 2, D, RW_DECAY_LORA), D ** -0.5),
        'rw_w2': nrm((n_c, 2, RW_DECAY_LORA, D), 0.1 * RW_DECAY_LORA ** -0.5),
        'rw_a0': nrm((n_c, 2, D), 0.1),
        'rw_a1': nrm((n_c, 2, D, RW_AAA_LORA), D ** -0.5),
        'rw_a2': nrm((n_c, 2, RW_AAA_LORA, D), RW_AAA_LORA ** -0.5),
        'rw_g1': nrm((n_c, D, RW_GATE_LORA), D ** -0.5),
        'rw_g2': nrm((n_c, RW_GATE_LORA, D), RW_GATE_LORA ** -0.5),
        'rw_k_k': 0.85 + nrm((n_c, D), 0.05),
        'rw_k_a': gain((n_c, D)),
        'rw_r_k': nrm((n_c, RW_HEADS, RW_HEAD), 0.1),
        'rw_ln_g': gain((n_c, D)),
        'rw_ln_b': nrm((n_c, D), 0.02),
    }

def first_block(x, c, ctx, c_ctx, ada_w, ada_b, norm_g, ffn_w_in, ffn_w_out,
              da_w_in, da_w_out, da_lambda, da_subln_g,
              na_w_in, na_w_out, na_rpb,
              rw_mu, rw_w_in, rw_w_out, rw_w0, rw_w1, rw_w2, rw_a0, rw_a1, rw_a2,
              rw_g1, rw_g2, rw_k_k, rw_k_a, rw_r_k, rw_ln_g, rw_ln_b):
    B, S, D = x.shape
    cos, sin = _axial_rope_tables(S)
    hx, hc = x, ctx
    silu_c, silu_cc = jax.nn.silu(c), jax.nn.silu(c_ctx)
    for i in range(DEPTH):
        last = i == DEPTH - 1
        kind, slot = i % N_MIXERS, i // N_MIXERS
        g = norm_g[i]
        mx = (silu_c @ ada_w[i] + ada_b[i]).reshape(B, N_MOD, 1, D)
        mc = (silu_cc @ ada_w[i] + ada_b[i]).reshape(N_MOD, D)

        hx = _ffn_sublayer(hx, (mx[:, 0], mx[:, 1], mx[:, 2]), g[0], g[1], ffn_w_in[i, 0], ffn_w_out[i, 0])
        hc = _ffn_sublayer(hc, (mc[0], mc[1], mc[2]), g[0], g[1], ffn_w_in[i, 0], ffn_w_out[i, 0])

        ux = _modulate(_rmsnorm(hx, g[2]), mx[:, 3], mx[:, 4])
        uc = _modulate(_rmsnorm(hc, g[2]), mc[3], mc[4])
        if kind == 0:
            lam_init = 0.8 - 0.6 * math.exp(-0.3 * i)
            yc, yx = _diff_attention(uc, ux, da_w_in[slot], da_w_out[slot], da_lambda[slot],
                                     da_subln_g[slot], lam_init, cos, sin, not last)
        elif kind == 1:
            yc, yx = _neighbourhood_attention(uc, ux, na_w_in[slot], na_w_out[slot], na_rpb[slot], not last)
        else:
            yc, yx = _rwkv7_mixer(uc, ux, rw_mu[slot], rw_w_in[slot], rw_w_out[slot],
                                  rw_w0[slot], rw_w1[slot], rw_w2[slot],
                                  rw_a0[slot], rw_a1[slot], rw_a2[slot],
                                  rw_g1[slot], rw_g2[slot], rw_k_k[slot], rw_k_a[slot],
                                  rw_r_k[slot], rw_ln_g[slot], rw_ln_b[slot], not last)
        hx = hx + mx[:, 5] * _rmsnorm(yx, g[3])

        hx = _ffn_sublayer(hx, (mx[:, 6], mx[:, 7], mx[:, 8]), g[4], g[5], ffn_w_in[i, 1], ffn_w_out[i, 1])
        if not last:
            hc = hc + mc[5] * _rmsnorm(yc, g[3])
            hc = _ffn_sublayer(hc, (mc[6], mc[7], mc[8]), g[4], g[5], ffn_w_in[i, 1], ffn_w_out[i, 1])
    return hx


RMS_EPS = 1e-6
Q_BLOCK = 128

MLA_HEADS = 4
MLA_NOPE = 64
MLA_ROPE = 32
MLA_V = 64
MLA_Q_LORA = 256
MLA_KV_LORA = 128
MLA_WIDTH = MLA_HEADS * MLA_V
ROPE_THETA = 10000.0

GDN_HEADS = 4
GDN_DK = 128
GDN_DV = 128
GDN_CONV = 4
GDN_CHUNK = 64
GDN_WIDTH = GDN_HEADS * GDN_DV

MOBA_HEADS = 4
MOBA_DH = 64
MOBA_BLOCK = 256
MOBA_TOPK = 3
MOBA_WIDTH = MOBA_HEADS * MOBA_DH

T5_BUCKETS = 32
T5_MAX_DIST = 2048

MIX_WIDTH = MLA_WIDTH + GDN_WIDTH + MOBA_WIDTH

IN_SIZES = (
    MLA_Q_LORA, MLA_KV_LORA, MLA_ROPE, MLA_WIDTH,
    GDN_HEADS * GDN_DK, GDN_HEADS * GDN_DK, GDN_WIDTH, GDN_WIDTH,
    GDN_HEADS, GDN_HEADS,
    MOBA_WIDTH, MOBA_WIDTH, MOBA_WIDTH, MOBA_WIDTH,
)
IN_COLS = sum(IN_SIZES)


def rmsnorm(x, w):
    xf = x.astype(jnp.float32)
    y = xf * lax.rsqrt(jnp.mean(xf * xf, axis=-1, keepdims=True) + RMS_EPS)
    return (y * w.astype(jnp.float32)).astype(x.dtype)

def l2norm(x):
    xf = x.astype(jnp.float32)
    return xf * lax.rsqrt(jnp.sum(xf * xf, axis=-1, keepdims=True) + 1e-6)

def rope_tables(seq, dim):
    inv = 1.0 / (ROPE_THETA ** (jnp.arange(0, dim, 2, dtype=jnp.float32) / dim))
    ang = jnp.arange(seq, dtype=jnp.float32)[:, None] * inv[None, :]
    return jnp.cos(ang), jnp.sin(ang)

def apply_rope(x, cos, sin):
    half = x.shape[-1] // 2
    xf = x.astype(jnp.float32)
    x1, x2 = xf[..., :half], xf[..., half:]
    c, s = cos[None, :, None, :], sin[None, :, None, :]
    return jnp.concatenate([x1 * c - x2 * s, x1 * s + x2 * c], axis=-1).astype(x.dtype)

def t5_bucket(rel):
    n = jnp.maximum(rel, 0)
    max_exact = T5_BUCKETS // 2
    nf = jnp.maximum(n, 1).astype(jnp.float32)
    large = max_exact + (jnp.log(nf / max_exact) / math.log(T5_MAX_DIST / max_exact)
                         * (T5_BUCKETS - max_exact)).astype(jnp.int32)
    large = jnp.minimum(large, T5_BUCKETS - 1)
    return jnp.where(n < max_exact, n, large)

def causal_block_attention(q, k, v, scale):
    B, S, H, Dk = q.shape
    Dv = v.shape[-1]
    nqb = S // Q_BLOCK
    qb = q.reshape(B, nqb, Q_BLOCK, H, Dk).transpose(1, 0, 2, 3, 4)
    kpos = jnp.arange(S)

    def one(args):
        i, qi = args
        logits = jnp.einsum('bqhd,bkhd->bhqk', qi, k, preferred_element_type=jnp.float32) * scale
        qpos = i * Q_BLOCK + jnp.arange(Q_BLOCK)
        logits = jnp.where(kpos[None, :] <= qpos[:, None], logits, -jnp.inf)
        p = jax.nn.softmax(logits, axis=-1).astype(v.dtype)
        return jnp.einsum('bhqk,bkhd->bqhd', p, v)

    out = lax.map(one, (jnp.arange(nqb), qb))
    return out.transpose(1, 0, 2, 3, 4).reshape(B, S, H, Dv)

def mla_mixer(c_q, c_kv, k_rope, q_norm_w, w_uq, kv_norm_w, w_ukv, cos, sin):
    B, S, _ = c_q.shape
    q = (rmsnorm(c_q, q_norm_w) @ w_uq).reshape(B, S, MLA_HEADS, MLA_NOPE + MLA_ROPE)
    q_nope, q_pe = q[..., :MLA_NOPE], q[..., MLA_NOPE:]
    q_pe = apply_rope(q_pe, cos, sin)
    kv = (rmsnorm(c_kv, kv_norm_w) @ w_ukv).reshape(B, S, MLA_HEADS, MLA_NOPE + MLA_V)
    k_nope, v = kv[..., :MLA_NOPE], kv[..., MLA_NOPE:]
    k_pe = apply_rope(k_rope[:, :, None, :], cos, sin)
    k = jnp.concatenate([k_nope, jnp.broadcast_to(k_pe, (B, S, MLA_HEADS, MLA_ROPE))], axis=-1)
    qh = jnp.concatenate([q_nope, q_pe], axis=-1)
    o = causal_block_attention(qh, k, v, (MLA_NOPE + MLA_ROPE) ** -0.5)
    return o.reshape(B, S, MLA_WIDTH)

def causal_conv(x, w):
    K = w.shape[0]
    S = x.shape[1]
    xp = jnp.pad(x, ((0, 0), (K - 1, 0), (0, 0)))
    return sum(xp[:, j:j + S] * w[j] for j in range(K))

def chunk_gated_delta_rule(q, k, v, beta, g):
    B, S, H, DK = q.shape
    DV = v.shape[-1]
    C = GDN_CHUNK
    N = S // C

    def chunks(t):
        return t.reshape(B, N, C, H, t.shape[-1]).transpose(0, 3, 1, 2, 4)

    qc, kc, vc = chunks(q), chunks(k), chunks(v)
    bc = beta.reshape(B, N, C, H).transpose(0, 3, 1, 2)
    gc = jnp.cumsum(g.reshape(B, N, C, H).transpose(0, 3, 1, 2), axis=-1)

    idx = jnp.arange(C)
    strict = idx[:, None] > idx[None, :]
    incl = idx[:, None] >= idx[None, :]
    diff = gc[..., :, None] - gc[..., None, :]
    decay = jnp.exp(jnp.where(incl, diff, -jnp.inf))

    kk = jnp.einsum('bhntd,bhnjd->bhntj', kc, kc)
    L = jnp.where(strict, bc[..., :, None] * kk * decay, 0.0)
    rhs = jnp.concatenate([kc * (bc * jnp.exp(gc))[..., None], vc * bc[..., None]], axis=-1)
    sol = lax.linalg.triangular_solve(L + jnp.eye(C, dtype=L.dtype), rhs,
                                      left_side=True, lower=True, unit_diagonal=True)
    W, U0 = sol[..., :DK], sol[..., DK:]
    A_qk = jnp.einsum('bhntd,bhnjd->bhntj', qc, kc) * decay
    q_g = qc * jnp.exp(gc)[..., None]
    k_end = kc * jnp.exp(gc[..., -1:] - gc)[..., None]
    g_end = jnp.exp(gc[..., -1])

    def step(state, xs):
        W_n, U0_n, A_n, qg_n, ke_n, ge_n = xs
        U = U0_n - jnp.einsum('bhcd,bhde->bhce', W_n, state)
        o = jnp.einsum('bhcd,bhde->bhce', qg_n, state) + jnp.einsum('bhtj,bhje->bhte', A_n, U)
        new_state = ge_n[..., None, None] * state + jnp.einsum('bhcd,bhce->bhde', ke_n, U)
        return new_state, o

    xs = tuple(jnp.moveaxis(t, 2, 0) for t in (W, U0, A_qk, q_g, k_end, g_end))
    s0 = jnp.zeros((B, H, DK, DV), jnp.float32)
    _, o = lax.scan(step, s0, xs)
    return o.transpose(1, 0, 3, 2, 4).reshape(B, S, H, DV)

def gdn_mixer(q, k, v, z, b, a, conv_w, A_log, dt_bias, norm_w):
    B, S, _ = q.shape
    qkv = jax.nn.silu(causal_conv(jnp.concatenate([q, k, v], axis=-1), conv_w))
    nk = GDN_HEADS * GDN_DK
    q, k, v = qkv[..., :nk], qkv[..., nk:2 * nk], qkv[..., 2 * nk:]
    q = l2norm(q.reshape(B, S, GDN_HEADS, GDN_DK)) * (GDN_DK ** -0.5)
    k = l2norm(k.reshape(B, S, GDN_HEADS, GDN_DK))
    v = v.reshape(B, S, GDN_HEADS, GDN_DV).astype(jnp.float32)
    beta = jax.nn.sigmoid(b.astype(jnp.float32))
    g = -jnp.exp(A_log.astype(jnp.float32)) * jax.nn.softplus(
        a.astype(jnp.float32) + dt_bias.astype(jnp.float32))
    o = chunk_gated_delta_rule(q, k, v, beta, g).astype(z.dtype)
    o = rmsnorm(o, norm_w) * jax.nn.silu(z.reshape(B, S, GDN_HEADS, GDN_DV))
    return o.reshape(B, S, GDN_WIDTH)

def moba_mixer(q, k, v, t5_table):
    B, S, _ = q.shape
    H, Dh, BS = MOBA_HEADS, MOBA_DH, MOBA_BLOCK
    q = q.reshape(B, S, H, Dh).transpose(0, 2, 1, 3)
    k = k.reshape(B, S, H, Dh).transpose(0, 2, 1, 3)
    v = v.reshape(B, S, H, Dh).transpose(0, 2, 1, 3)
    NB = -(-S // BS)
    pad = NB * BS - S
    kp = jnp.pad(k, ((0, 0), (0, 0), (0, pad), (0, 0)))
    vp = jnp.pad(v, ((0, 0), (0, 0), (0, pad), (0, 0)))
    kblk = kp.reshape(B, H, NB, BS, Dh)
    vblk = vp.reshape(B, H, NB, BS, Dh)
    kmean = jnp.mean(kblk.astype(jnp.float32), axis=3).astype(k.dtype)
    topk = min(MOBA_TOPK, NB)
    scale = Dh ** -0.5
    nqb = S // Q_BLOCK
    qb = jnp.moveaxis(q.reshape(B, H, nqb, Q_BLOCK, Dh), 2, 0)
    bi = jnp.arange(B)[:, None, None, None]
    hi = jnp.arange(H)[None, :, None, None]
    hi5 = jnp.arange(H)[None, :, None, None, None]
    blk_iota = jnp.arange(BS)

    def one(args):
        i, qi = args
        qpos = i * Q_BLOCK + jnp.arange(Q_BLOCK)
        own = (i * Q_BLOCK) // BS
        gate = jnp.einsum('bhqd,bhnd->bhqn', qi, kmean, preferred_element_type=jnp.float32)
        gate = jnp.where(jnp.arange(NB) < own, gate, -jnp.inf)
        _, sel = lax.top_k(gate, topk)
        valid = sel < own
        ksel = kblk[bi, hi, sel]
        vsel = vblk[bi, hi, sel]
        kpos_sel = sel[..., None] * BS + blk_iota
        bias_sel = t5_table[t5_bucket(qpos[None, None, :, None, None] - kpos_sel), hi5]
        l_sel = jnp.einsum('bhqd,bhqnkd->bhqnk', qi, ksel, preferred_element_type=jnp.float32) * scale
        l_sel = jnp.where(valid[..., None], l_sel + bias_sel.astype(jnp.float32), -jnp.inf)
        kown = lax.dynamic_slice_in_dim(kp, own * BS, BS, axis=2)
        vown = lax.dynamic_slice_in_dim(vp, own * BS, BS, axis=2)
        kpos_own = own * BS + blk_iota
        rel_own = qpos[:, None] - kpos_own[None, :]
        bias_own = t5_table[t5_bucket(rel_own)].transpose(2, 0, 1)[None]
        l_own = jnp.einsum('bhqd,bhkd->bhqk', qi, kown, preferred_element_type=jnp.float32) * scale
        l_own = jnp.where(rel_own[None, None] >= 0, l_own + bias_own.astype(jnp.float32), -jnp.inf)
        logits = jnp.concatenate([l_sel.reshape(B, H, Q_BLOCK, topk * BS), l_own], axis=-1)
        p = jax.nn.softmax(logits, axis=-1).astype(v.dtype)
        p_sel = p[..., :topk * BS].reshape(B, H, Q_BLOCK, topk, BS)
        p_own = p[..., topk * BS:]
        return (jnp.einsum('bhqnk,bhqnkd->bhqd', p_sel, vsel)
                + jnp.einsum('bhqk,bhkd->bhqd', p_own, vown))

    out = lax.map(one, (jnp.arange(nqb), qb))
    out = out.transpose(1, 2, 0, 3, 4).reshape(B, H, S, Dh)
    return out.transpose(0, 2, 1, 3).reshape(B, S, MOBA_WIDTH)

def hybrid_layer(x, norm_w, w_in, mla_q_norm, mla_w_uq, mla_kv_norm, mla_w_ukv,
                 gdn_conv_w, gdn_A_log, gdn_dt_bias, gdn_norm_w, w_out, t5_table, cos, sin):
    h = rmsnorm(x, norm_w)
    proj = h @ w_in
    split_points = np.cumsum(IN_SIZES)[:-1].tolist()
    (m_cq, m_ckv, m_kr, m_gate, g_q, g_k, g_v, g_z, g_b, g_a,
     c_q, c_k, c_v, c_gate) = jnp.split(proj, split_points, axis=-1)
    y_mla = mla_mixer(m_cq, m_ckv, m_kr, mla_q_norm, mla_w_uq, mla_kv_norm, mla_w_ukv,
                      cos, sin) * jax.nn.silu(m_gate)
    y_gdn = gdn_mixer(g_q, g_k, g_v, g_z, g_b, g_a, gdn_conv_w, gdn_A_log, gdn_dt_bias, gdn_norm_w)
    y_moba = moba_mixer(c_q, c_k, c_v, t5_table) * jax.nn.silu(c_gate)
    y = jnp.concatenate([y_mla, y_gdn, y_moba], axis=-1)
    return x + y @ w_out

def second_inputs(seed: int = 0) -> dict:
    key = jax.random.key(seed)
    ks = jax.random.split(key, 20)
    nrm = jax.random.normal
    f32 = jnp.float32
    dt = jnp.exp(jax.random.uniform(ks[10], (DEPTH, GDN_HEADS), f32, math.log(1e-3), math.log(1e-1)))
    return {
        "x": nrm(ks[0], (BATCH, SEQ, D_MODEL), f32),
        "norm_w": 1.0 + 0.02 * nrm(ks[1], (DEPTH, D_MODEL), f32),
        "w_in": nrm(ks[2], (DEPTH, D_MODEL, IN_COLS), f32) * D_MODEL ** -0.5,
        "mla_q_norm": 1.0 + 0.02 * nrm(ks[3], (DEPTH, MLA_Q_LORA), f32),
        "mla_w_uq": nrm(ks[4], (DEPTH, MLA_Q_LORA, MLA_HEADS * (MLA_NOPE + MLA_ROPE)), f32) * MLA_Q_LORA ** -0.5,
        "mla_kv_norm": 1.0 + 0.02 * nrm(ks[5], (DEPTH, MLA_KV_LORA), f32),
        "mla_w_ukv": nrm(ks[6], (DEPTH, MLA_KV_LORA, MLA_HEADS * (MLA_NOPE + MLA_V)), f32) * MLA_KV_LORA ** -0.5,
        "gdn_conv_w": nrm(ks[7], (DEPTH, GDN_CONV, 2 * GDN_HEADS * GDN_DK + GDN_WIDTH), f32) * GDN_CONV ** -0.5,
        "gdn_A_log": jnp.log(jax.random.uniform(ks[8], (DEPTH, GDN_HEADS), f32, 1.0, 16.0)),
        "gdn_dt_bias": jnp.log(jnp.expm1(dt)),
        "gdn_norm_w": 1.0 + 0.02 * nrm(ks[9], (DEPTH, GDN_DV), f32),
        "w_out": nrm(ks[11], (DEPTH, MIX_WIDTH, D_MODEL), f32) * (MIX_WIDTH * 2 * DEPTH) ** -0.5,
        "t5_table": 0.5 * nrm(ks[12], (T5_BUCKETS, MOBA_HEADS), f32),
        "final_norm_w": 1.0 + 0.02 * nrm(ks[13], (D_MODEL,), f32),
    }

def second_block(x, norm_w, w_in, mla_q_norm, mla_w_uq, mla_kv_norm, mla_w_ukv,
              gdn_conv_w, gdn_A_log, gdn_dt_bias, gdn_norm_w, w_out, t5_table, final_norm_w):
    S = x.shape[1]
    cos, sin = rope_tables(S, MLA_ROPE)
    for l in range(DEPTH):
        x = hybrid_layer(x, norm_w[l], w_in[l], mla_q_norm[l], mla_w_uq[l], mla_kv_norm[l],
                         mla_w_ukv[l], gdn_conv_w[l], gdn_A_log[l], gdn_dt_bias[l],
                         gdn_norm_w[l], w_out[l], t5_table, cos, sin)
    return rmsnorm(x, final_norm_w)


def setup_inputs(seed=0):
    out = dict(first_inputs(seed))
    for name, value in second_inputs(seed + 1).items():
        if name != "x":
            out[name + "_2"] = value
    return out


def reference(
    x, c, ctx, c_ctx, ada_w, ada_b, norm_g, ffn_w_in, ffn_w_out, da_w_in, da_w_out, da_lambda,
    da_subln_g, na_w_in, na_w_out, na_rpb, rw_mu, rw_w_in, rw_w_out, rw_w0, rw_w1, rw_w2, rw_a0,
    rw_a1, rw_a2, rw_g1, rw_g2, rw_k_k, rw_k_a, rw_r_k, rw_ln_g, rw_ln_b, norm_w_2, w_in_2,
    mla_q_norm_2, mla_w_uq_2, mla_kv_norm_2, mla_w_ukv_2, gdn_conv_w_2, gdn_A_log_2,
    gdn_dt_bias_2, gdn_norm_w_2, w_out_2, t5_table_2, final_norm_w_2,
):
    x = first_block(
        x, c, ctx, c_ctx, ada_w, ada_b, norm_g, ffn_w_in, ffn_w_out, da_w_in, da_w_out,
        da_lambda, da_subln_g, na_w_in, na_w_out, na_rpb, rw_mu, rw_w_in, rw_w_out, rw_w0,
        rw_w1, rw_w2, rw_a0, rw_a1, rw_a2, rw_g1, rw_g2, rw_k_k, rw_k_a, rw_r_k, rw_ln_g,
        rw_ln_b,
    )
    return second_block(
        x, norm_w_2, w_in_2, mla_q_norm_2, mla_w_uq_2, mla_kv_norm_2, mla_w_ukv_2, gdn_conv_w_2,
        gdn_A_log_2, gdn_dt_bias_2, gdn_norm_w_2, w_out_2, t5_table_2, final_norm_w_2,
    )


_drawn_inputs = setup_inputs


def setup_inputs(seed=0):
    import zlib

    import numpy as np

    out = dict(_drawn_inputs(seed))
    spreads = {}
    factors = {'da_subln_g': 3.15,
     'na_rpb': 5.884,
     'norm_w_2': 6.126,
     'mla_q_norm_2': 8.0,
     'mla_kv_norm_2': 8.0,
     'gdn_norm_w_2': 8.0,
     't5_table_2': 3.663,
     'final_norm_w_2': 2.808}
    for name, (base, spread) in spreads.items():
        noise = np.random.default_rng([zlib.crc32(name.encode()), seed]).standard_normal(out[name].shape)
        drawn = base * np.exp(spread * noise) if base else spread * noise
        out[name] = __import__('jax').numpy.asarray(drawn.astype(out[name].dtype))
    for name, factor in factors.items():
        out[name] = (out[name] * factor).astype(out[name].dtype)
    return out
```

```python
from contextlib import ExitStack, contextmanager

import numpy as np

import concourse.bass as bass
from concourse import mybir

F32 = mybir.dt.float32
ALU = mybir.AluOpType
ACT = mybir.ActivationFunctionType
AX = mybir.AxisListType

P = 128
D = 1024
DC = D // P
CTX, SEQ = 256, 256
T = CTX + SEQ
TT = T // P
LAYERS = 2
N_MOD = 9
F = 2816
FC = F // P
EPS = 1e-6
GRID_W = 64
ROWS = SEQ // GRID_W
NA_ROWS, NA_COLS = 8, 16
NA_H = 16
RPB_R, RPB_C = 2 * NA_ROWS - 1, 2 * NA_COLS - 1
SPAN = (ROWS - 1) * RPB_C + GRID_W
LAM_INIT = 0.2
NEG = -1e30
IN2 = 3752
MLA_H, NOPE, ROPE, MLA_QK = 4, 64, 32, 96
GH = 4
GN = GH * (SEQ // P)
LEVELS = 7
CONV = 4
TAB = 384
PAD = CONV - 1


CONST_COLS = {}


def _constants():
    f = np.float32
    i = np.arange(P)
    parts = {}
    parts["ident"] = np.eye(P, dtype=f)
    parts["flip"] = np.eye(P, dtype=f)[::-1]
    parts["ones"] = np.ones((P, P), f)
    parts["upto"] = (i[:, None] <= i[None, :]).astype(f)
    parts["future"] = np.where(i[None, :] >= i[:, None], 0.0, NEG).astype(f)
    parts["strict"] = (i[None, :] > i[:, None]).astype(f)
    low = []
    for m in range(LEVELS):
        b = 2 ** m
        tb, jb = i[:, None] // b, i[None, :] // b
        low.append(((tb // 2 == jb // 2) & (tb % 2 == 1) & (jb % 2 == 0)).astype(f))
    parts["low0"] = low[0]
    parts["lowT"] = np.concatenate([x.T for x in low], axis=1)
    d = np.arange(P)
    rot = np.zeros((P, P), f)
    for m in range(P):
        if (m // 16) % 2 == 0:
            rot[m + 16, m] = -1
        else:
            rot[m - 16, m] = 1
    parts["rot"] = rot
    tok = np.arange(SEQ)
    pos = np.stack([tok // GRID_W, tok % GRID_W], -1).astype(f)
    freq = (np.float32(10000.0) ** (-np.arange(16, dtype=f) / 16)).astype(f)
    ang = pos[:, :, None] * freq
    a = ang[:, (d // 32) % 2, d % 16].T
    parts["cos"], parts["sin"] = np.cos(a).astype(f), np.sin(a).astype(f)
    r96 = np.zeros((P, MLA_QK), f)
    for m in range(NOPE, MLA_QK):
        if m < NOPE + 16:
            r96[m + 16, m] = -1
        else:
            r96[m - 16, m] = 1
    parts["rot96"] = r96
    inv = (1.0 / (np.float32(10000.0) ** (np.arange(0, ROPE, 2, dtype=f) / ROPE))).astype(f)
    a2 = (tok.astype(f)[:, None] * inv[None, :]).T
    c96, s96 = np.ones((P, SEQ), f), np.zeros((P, SEQ), f)
    for m in range(NOPE, MLA_QK):
        c96[m], s96[m] = np.cos(a2[(m - NOPE) % 16]), np.sin(a2[(m - NOPE) % 16])
    parts["cos96"], parts["sin96"] = c96, s96
    qc = (GRID_W - 1) - (i % GRID_W)
    start = np.clip(qc - NA_COLS // 2, 0, GRID_W - NA_COLS)
    kc = np.arange(GRID_W)
    win = (kc[None, :] >= start[:, None]) & (kc[None, :] < start[:, None] + NA_COLS)
    parts["win"] = win.astype(f)
    parts["notwin"] = np.where(win, 0.0, -1e9).astype(f)
    n = (SEQ - 1) - np.arange(TAB)
    nf = np.maximum(n, 1).astype(f)
    large = 16 + (np.log(nf / 16) / np.log(f(2048 / 16)) * 16).astype(np.int32)
    bucket = np.where(n < 16, np.maximum(n, 0), np.minimum(large, 31))
    hot = np.zeros((P, TAB), f)
    hot[bucket[n >= 0], np.nonzero(n >= 0)[0]] = 1.0
    hot[32, n < 0] = NEG
    parts["hot"] = hot
    at = 0
    for k, v in parts.items():
        CONST_COLS[k] = (at, at + v.shape[1])
        at += v.shape[1]
    return np.ascontiguousarray(np.concatenate(list(parts.values()), axis=1))


CONSTS = _constants()


class Tally:

    def __init__(self):
        self.n, self.term = 0, None

    def up(self, k=1):
        self.n += k
        return self.now()

    def now(self):
        return self.n if self.term is None else self.term + self.n


class Banks(Tally):

    def __init__(self, first, count):
        super().__init__()
        self.first, self.count, self.turn = first, count, None

    def take(self):
        bank = self.first + self.n % self.count
        free = self.n // self.count
        if self.turn is not None:
            free = self.turn + free
        return bank, self.up(), free


@contextmanager
def repeat(eng, turns, *tallies):
    with eng.Fori(0, turns) as i:
        before = [t.n for t, _ in tallies]
        for t, per in tallies:
            t.term = i * per
            if isinstance(t, Banks):
                assert per % t.count == 0
                t.turn = i * (per // t.count)
        yield i
        for (t, per), b in zip(tallies, before):
            assert t.n - b == per, (t.n - b, per)
            t.term = None
            if isinstance(t, Banks):
                t.turn = None
            t.n = b + per * turns


def build(nc, A, out, const, tab_dram, dbg=None, stop=None):
    with ExitStack() as ctx:
        def sb(name, shape):
            return ctx.enter_context(nc.sbuf_tensor(name, shape, F32))

        def sem(name):
            return ctx.enter_context(nc.semaphore(name))

        psum = [ctx.enter_context(nc.psum_tensor(f"bank{b}", [P, 512], F32)) for b in range(8)]
        hT = sb("hT", [P, DC, T])
        uT = sb("uT", [P, DC, T])
        big = sb("big", [P, 24 * T])
        yT = sb("yT", [P, DC, T])
        wring = sb("wring", [P, 2, FC * P])
        cst = sb("cst", [P, CONSTS.shape[1]])
        vraw = sb("vraw", [P, 4, P])
        vec = sb("vec", [P, 4, P])
        sc = sb("sc", [P, DC, 2])
        mod = sb("mod", [P, LAYERS, N_MOD * DC, 2])
        coefA = sb("coefA", [P, 6, DC, 2])
        coefG = sb("coefG", [P, 6, DC, 2])
        lamv = sb("lamv", [P, 4 * 64])
        lams = sb("lams", [P, 8])
        stat = sb("stat", [P, 2, 32])
        diag = sb("diag", [P, T])
        half = sb("half", [P, 2, T])
        rawb = sb("rawb", [P, 2, NA_H, SPAN])
        maskb = sb("maskb", [P, 2, SEQ])
        prob = sb("prob", [P, 2, 2, T])
        probn = sb("probn", [P, 2, T])
        probT = sb("probT", [P, 2, TT, P])
        negm = sb("negm", [P, 2, 2, 2])
        rsum = sb("rsum", [P, 2, 2, 2])
        brev = sb("brev", [P, 5, SEQ])
        t5w = sb("t5w", [33, 5])
        tline = sb("tline", [5, TAB])
        wuq = sb("wuq", [P, LAYERS, 2, MLA_H * MLA_QK])
        wukv = sb("wukv", [P, LAYERS, 512])
        galog = sb("galog", [P, LAYERS, 2, GH])
        gs = sb("gs", [P, 16, GN])
        fin = yT

        def c(name):
            a, b = CONST_COLS[name]
            return cst[:, a:b]

        bigc = big[:, :].rearrange("p (c t) -> p c t", t=T)
        vtok = big[:, 16 * T:24 * T].rearrange("p (m n) -> p m n", n=D)
        adaw = big[:, :].rearrange("p (s k n) -> p s k n", s=3, k=DC)
        stage = yT[:, :, :].rearrange("p a b -> p (a b)").rearrange("p (m n) -> p m n", n=D)
        at = [0]

        def piece(store, n):
            at[0] += n
            return store[:, at[0] - n:at[0]]

        def three(ap, m):
            return ap.rearrange("p (m n) -> p m n", m=m)

        convin = three(piece(big, 12 * (SEQ + 4)), 12)
        gz = three(piece(big, 4 * SEQ), 4)
        mgate = three(piece(big, 2 * SEQ), 2)
        cgate = three(piece(big, 2 * SEQ), 2)
        attn0 = at[0]
        mbq = three(piece(big, 2 * SEQ), 2)
        mbk = three(piece(big, 2 * SEQ), 2)
        mbv = three(piece(big, 2 * SEQ), 2)
        cq = three(piece(big, 2 * SEQ), 2)
        ckv = piece(big, SEQ)
        mq = three(piece(big, MLA_H * SEQ), MLA_H)
        mk = three(piece(big, MLA_H * SEQ), MLA_H)
        mv = three(piece(big, 2 * 256), 2)
        attn1 = at[0]
        yc = three(piece(big, DC * SEQ), DC)
        assert at[0] <= 24 * T
        at[0] = 0
        ktok = three(piece(big, GN * P), GN)
        vtk = three(piece(big, GN * P), GN)
        at[0] = attn0
        cvo = three(piece(big, 12 * SEQ), 12)
        EG = three(piece(big, GH * P), GH)
        qg = EG
        S1 = three(piece(big, GH * P), GH)
        assert at[0] <= attn1
        DTm, ATm = hT[:, :, 0:P], hT[:, :, P:2 * P]
        at[0] = 0
        yflat = yT[:, :, :].rearrange("p a b -> p (a b)")
        Xm = three(piece(yflat, GN * P), GN)
        XT = three(piece(yflat, GN * P), GN)
        Ym = three(piece(yflat, GN * P), GN)
        LT = three(piece(yflat, GN * P), GN)
        rflat = rawb[:, :, :, :].rearrange("p a b c -> p (a b c)")
        at[0] = 0
        LmT = three(piece(rflat, GN * P), GN)
        gB = three(piece(rflat, GN * P), GN)
        Rm = three(piece(rflat, GN * P), GN)
        Um = three(piece(rflat, GN * P), GN)
        prt = prob[:, :, :, :].rearrange("p a b t -> p (a b t)")
        convt = prt[:, 0:2048]
        oraw = three(prt[:, 0:GH * SEQ], GH)

        def v_norm(l, g):
            return vec[:, 0, (l * 6 + g) * DC:(l * 6 + g + 1) * DC]

        V_C, V_CC, V_NW = 96, 104, 112
        V_FIN, V_SUB, V_Q, V_KV, V_GN = 72, 80, 81, 85, 87

        x_in = sem("x_in")
        const_in = sem("const_in")
        vec_in = sem("vec_in")
        misc_in = sem("misc_in")
        rawb_in = sem("rawb_in")
        ada_in = [sem(f"ada_in{s}") for s in range(3)]
        w_in = [sem(f"w_in{s}") for s in range(2)]
        line_out = sem("line_out")
        brev_in = sem("brev_in")
        out_done = sem("out_done")
        gemm_full = sem("gemm_full")
        gemm_free = [sem(f"gemm_free{b}") for b in range(4)]
        ada_done = sem("ada_done")
        small_full = sem("small_full")
        small_free = [sem(f"small_free{b}") for b in range(2)]
        pv_done = sem("pv_done")
        o_taken = sem("o_taken")
        vec_step = sem("vec_step")
        act_step = sem("act_step")
        pool_step = sem("pool_step")
        t5_set = sem("t5_set")
        h_ready = sem("h_ready")
        vec_ready = sem("vec_ready")
        sc_ready = sem("sc_ready")
        line_ready = sem("line_ready")
        sq_ready = sem("sq_ready")
        var_ready = sem("var_ready")
        root_ready = sem("root_ready")
        diag_ready = sem("diag_ready")
        n_ready = sem("n_ready")
        u_ready = sem("u_ready")
        silu_ready = sem("silu_ready")
        silu_used = sem("silu_used")
        g_ready = sem("g_ready")
        y_ready = sem("y_ready")
        qkv_ready = sem("qkv_ready")
        rope_ready = sem("rope_ready")
        bias_ready = sem("bias_ready")
        negm_ready = sem("negm_ready")
        exp_ready = sem("exp_ready")
        probn_ready = sem("probn_ready")
        probT_ready = sem("probT_ready")
        o_ready = sem("o_ready")
        lam_in = sem("lam_in")
        lam_exp = sem("lam_exp")
        out_ready = sem("out_ready")
        a_act = sem("a_act")
        v_hyb = sem("v_hyb")

        v_ready = sem("v_ready")
        on_ready = sem("on_ready")
        block = ctx.enter_context(nc.Block())

        def da_items():
            for h in range(8):
                for t in range(TT):
                    nk = CTX if t < CTX // P else T
                    yield dict(
                        q=[bigc[64 * j:64 * j + 64, h, t * P:t * P + P] for j in range(2)],
                        k=[bigc[64 * j:64 * j + 64, 8 + h, 0:nk] for j in range(2)], nk=nk, scale=0.125,
                        v=[vtok[:, kt, h * P:h * P + P] for kt in range(nk // P)], rows=(0, P), cols=t * P)

        def na_items():
            for h in range(NA_H):
                r = 64 * (h % 2)
                for t in range(SEQ // P):
                    yield dict(
                        q=[bigc[r:r + 64, h // 2, CTX + t * P:CTX + t * P + P]], k=[bigc[r:r + 64, 8 + h // 2, :]],
                        nk=T, scale=1.0, na=(h, t),
                        v=[vtok[:, kt, h * 64:h * 64 + 64] for kt in range(TT)], rows=(r, r + 64), cols=t * P)

        def mla_items():
            for h in range(MLA_H):
                r = 64 * (h % 2)
                for t in range(2):
                    nk = (t + 1) * P
                    yield dict(q=[mq[0:MLA_QK, h, t * P:t * P + P]], k=[mk[0:MLA_QK, h, 0:nk]], nk=nk, scale=1.0,
                               bias=brev[:, 4, P * (1 - t):P * (1 - t) + nk],
                               v=[mv[:, kt, h * 64:h * 64 + 64] for kt in range(t + 1)], rows=(r, r + 64), cols=t * P)

        def moba_items():
            for h in range(4):
                r = 64 * (h % 2)
                for t in range(2):
                    nk = (t + 1) * P
                    yield dict(q=[mbq[r:r + 64, h // 2, t * P:t * P + P]], k=[mbk[r:r + 64, h // 2, 0:nk]], nk=nk,
                               scale=1.0, bias=brev[:, h, P * (1 - t):P * (1 - t) + nk],
                               v=[mbv[:, kt, h * 64:h * 64 + 64] for kt in range(t + 1)], rows=(r, r + 64),
                               cols=t * P)

        def item_base(counter, n):
            counter[0] += n
            return counter[0] - n

        HY = [(0, 256), (256, 160), (416, 256)] + [(672 + 256 * b, 256) for b in range(8)] + \
             [(2720, 264), (2984, 256), (3240, 256), (3496, 256)]

        STAGES = ["ada", "ffn00", "da", "ffn01", "ffn10", "na", "ffn11", "hy0", "hy1"]
        run = STAGES if stop is None else STAGES[:STAGES.index(stop) + 1]

        @block.sync
        def _(sp):
            sp.dma_start(cst[:, :], const).then_inc(const_in, 16)
            sp.dma_start(stage[:, 0:2, :], A["ctx"][0].rearrange("(m p) n -> p m n", p=P)).then_inc(x_in, 16)
            sp.dma_start(stage[:, 2:4, :], A["x"][0].rearrange("(m p) n -> p m n", p=P)).then_inc(x_in, 16)
            rows = [(0, 0, A["norm_g"].rearrange("l g (c p) -> (l g c) p", p=P)),
                    (0, V_C, A["c"].rearrange("o (c p) -> (o c) p", p=P)),
                    (0, V_CC, A["c_ctx"].rearrange("(c p) -> c p", p=P)),
                    (0, V_NW, A["norm_w_2"].rearrange("l (c p) -> (l c) p", p=P)),
                    (1, 0, A["ada_b"][0].rearrange("(c p) -> c p", p=P)),
                    (2, 0, A["ada_b"][1].rearrange("(c p) -> c p", p=P)),
                    (1, V_FIN, A["final_norm_w_2"].rearrange("(c p) -> c p", p=P)),
                    (1, V_SUB, A["da_subln_g"]),
                    (1, V_Q, A["mla_q_norm_2"].rearrange("l (c p) -> (l c) p", p=P)),
                    (1, V_KV, A["mla_kv_norm_2"]),
                    (1, V_GN, A["gdn_norm_w_2"]),
                    (3, 0, A["gdn_conv_w_2"].rearrange("l j (c p) -> (l j c) p", p=P))]
            for tile, r, src in rows:
                sp.dma_start(vraw[r:r + src.shape[0], tile, :], src).then_inc(vec_in, 16)
            views = [A["ada_w"][l].rearrange("(k p) n -> p k n", p=P) for l in range(LAYERS)]
            done = Tally()
            for l in range(LAYERS):
                if l == 0:
                    for s in range(3):
                        sp.dma_start(adaw[:, s], views[0][:, :, s * 512:(s + 1) * 512]).then_inc(ada_in[s], 16)
                    sp.dma_start(lamv[:, :], A["da_lambda"][0].rearrange("(o a) b -> o (a b)", o=1).to_broadcast([P, 256])).then_inc(lam_in, 16)
                    sp.dma_start(t5w[0:32, 0:4], A["t5_table_2"]).then_inc(misc_in, 16)
                    for k in range(LAYERS):
                        sp.dma_start(wuq[:, k], A["mla_w_uq_2"][k].rearrange("(a p) n -> p a n", p=P)).then_inc(misc_in, 16)
                        sp.dma_start(wukv[:, k], A["mla_w_ukv_2"][k]).then_inc(misc_in, 16)
                        sp.dma_start(galog[:, k, 0], A["gdn_A_log_2"][k:k + 1, :].to_broadcast([P, GH])).then_inc(misc_in, 16)
                        sp.dma_start(galog[:, k, 1], A["gdn_dt_bias_2"][k:k + 1, :].to_broadcast([P, GH])).then_inc(misc_in, 16)
                    for t in range(2):
                        base = A["na_rpb"][0, 0, 0, 0:1]
                        for rr in range(2):
                            r = 2 * t + 1 - rr
                            src = bass.AP(tensor=base.tensor, offset=base.offset + (NA_ROWS - 1 - r) * RPB_C + NA_COLS - GRID_W,
                                          ap=[[1, GRID_W], [RPB_R * RPB_C, NA_H], [1, SPAN]])
                            sp.dma_start(rawb[64 * rr:64 * rr + 64, t], src).then_inc(rawb_in, 16)
                first = 1 if l == 0 else 0
                if l == 0:
                    done.n = 0
                with sp.Fori(first, 6) as i:
                    for s in range(3):
                        sp.wait_ge(ada_done, (i * 3 + (18 * l - 2 + s)))
                        sp.dma_start(adaw[:, s], views[l][:, :, bass.ds(i * 1536 + s * 512, 512)]).then_inc(ada_in[s], 16)

            gem = Tally()
            gem.up(DC)
            last = [0, 0]

            def blocks(n, per, load):
                for s in range(2):
                    if last[s]:
                        sp.wait_ge(gemm_full, last[s])
                    load(0, s, s)
                if n > 2:
                    base = gem.n
                    with sp.Fori(1, n // 2) as i:
                        for s in range(2):
                            sp.wait_ge(gemm_full, i * (2 * per) + (base + per * (s + 1) - 2 * per))
                            load(i, s, i * 2 + s)
                gem.up(n * per)
                last[0], last[1] = gem.n - per, gem.n

            def load_ffn(l, s_, T_):
                w1 = A["ffn_w_in"][l, s_].rearrange("(k p) n -> p k n", p=P)
                w2 = A["ffn_w_out"][l, s_].rearrange("(k p) n -> p k n", p=P)

                def up(i, s, b):
                    slot = wring[:, s, 0:DC * 2 * P].rearrange("p (k a n) -> p k a n", k=DC, a=2)
                    for a in range(2):
                        src = w1[:, :, bass.ds(b * P + a * F, P)] if not isinstance(b, int) else w1[:, :, b * P + a * F:b * P + a * F + P]
                        sp.dma_start(slot[:, :, a], src).then_inc(w_in[s], 16)

                def down(i, s, b):
                    slot = wring[:, s, :].rearrange("p (k n) -> p k n", k=FC)
                    for a in range(2):
                        r = slice(a * FC // 2, (a + 1) * FC // 2)
                        src = w2[:, r, bass.ds(b * P, P)] if not isinstance(b, int) else w2[:, r, b * P:b * P + P]
                        sp.dma_start(slot[:, r], src).then_inc(w_in[s], 16)

                blocks(FC, 2, up)
                blocks(DC, 1, down)

            def load_cols(view, width=256):
                def load(i, s, b):
                    slot = wring[:, s, 0:DC * width].rearrange("p (k n) -> p k n", k=DC)
                    for a in range(2):
                        r = slice(a * DC // 2, (a + 1) * DC // 2)
                        src = view[:, r, bass.ds(b * width, width)] if not isinstance(b, int) else view[:, r, b * width:(b + 1) * width]
                        sp.dma_start(slot[:, r], src).then_inc(w_in[s], 16)
                return load

            for st in run:
                if st == "ada":
                    sp.wait_ge(line_ready, 1)
                    sp.dma_start(tab_dram, tline[:, :]).then_inc(line_out, 16)
                    sp.wait_ge(line_out, 16)
                    src = bass.AP(tensor=tab_dram.tensor, offset=tab_dram.offset, ap=[[1, P], [TAB, 5], [1, SEQ]])
                    sp.dma_start(brev[:, :, :], src).then_inc(brev_in, 16)
                elif st.startswith("ffn"):
                    load_ffn(int(st[3]), int(st[4]), T)
                elif st in ("da", "na"):
                    w = A[st + "_w_in"][0].rearrange("(k p) n -> p k n", p=P)
                    blocks(4, 2, load_cols(w[:, :, 0:D]))
                    blocks(4, 2, load_cols(w[:, :, D:2 * D]))
                    blocks(4, 4, load_cols(w[:, :, 2 * D:3 * D]))
                    gem.up(64 if st == "da" else 32)
                    blocks(4, 2, load_cols(A[st + "_w_out"][0].rearrange("(k p) n -> p k n", p=P)))
                else:
                    l = int(st[2])
                    w = A["w_in_2"][l].rearrange("(k p) n -> p k n", p=P)
                    for n, (c0, width) in enumerate(HY):
                        s = (19 * l + n) % 2
                        sp.wait_ge(gemm_full, last[s])
                        slot = wring[:, s, 0:DC * width].rearrange("p (k n) -> p k n", k=DC)
                        for a in range(2):
                            r = slice(a * DC // 2, (a + 1) * DC // 2)
                            sp.dma_start(slot[:, r], w[:, r, c0:c0 + width]).then_inc(w_in[s], 16)
                        gem.up(2 if n == 11 else 1)
                        last[s] = gem.n
                    gem.up(6 + 16 + (4 + 2 + 4 + 2 + 2) + (6 * (LEVELS - 2) + 4) + 6)
                    w_o = A["w_out_2"][l].rearrange("(k p) n -> p k n", p=P)
                    for b in range(4):
                        s = (19 * l + len(HY) + b) % 2
                        sp.wait_ge(gemm_full, last[s])
                        slot = wring[:, s, 0:DC * 256].rearrange("p (k n) -> p k n", k=DC)
                        for a in range(2):
                            r = slice(a * DC // 2, (a + 1) * DC // 2)
                            sp.dma_start(slot[:, r], w_o[:, r, b * 256:(b + 1) * 256]).then_inc(w_in[s], 16)
                        gem.up(1)
                        last[s] = gem.n
            sp.wait_ge(out_ready, 1)
            if dbg is not None:
                sp.wait_ge(out_ready, 2)
                sp.dma_start(dbg, hT[:, :, :]).then_inc(out_done, 16)
                sp.wait_ge(out_done, 16)
            if stop is None:
                sp.dma_start(out[0].rearrange("(m p) n -> p m n", p=P), stage[:, 0:2, :]).then_inc(out_done, 16)
                sp.wait_ge(out_done, 16)

        def rep(ap, m):
            return bass.AP(tensor=ap.tensor, offset=ap.offset, ap=[ap.ap[0], [0, m], ap.ap[1]])

        def wide(ap, m):
            return bass.AP(tensor=ap.tensor, offset=ap.offset, ap=[ap.ap[0], ap.ap[1], [0, m]])

        def shape_of(st):
            return (CTX, [1]) if st in ("ffn11", "na") else (0, [0, 1])

        SUB = {"ffn00": (0, 0), "da": (0, 1), "ffn01": (0, 2), "ffn10": (1, 0), "na": (1, 1), "ffn11": (1, 2)}
        ident, flip, ones, upto = c("ident"), c("flip"), c("ones"), c("upto")
        STEPS = MLA_QK ** -0.5

        @block.tensor
        def _(pe):
            gemm, small, opsum = Banks(0, 4), Banks(4, 2), Banks(6, 2)
            w_t = [Tally(), Tally()]
            tl = {k: Tally() for k in ("u", "g", "sq", "diag", "qkv", "v", "probn", "probT", "bias", "on", "vh",
                                       "aa", "adaw")}
            mm = nc.tensor.matmul

            def bank(pool, frees):
                b, full, free = pool.take()
                if not (isinstance(free, int) and free == 0):
                    pe.wait_ge(frees[b - pool.first], free)
                return psum[b]

            def gbank():
                return bank(gemm, gemm_free)

            def sbank():
                return bank(small, small_free)

            def stats(groups, nt):
                o = sbank()
                for g, parts in enumerate(groups):
                    for t in range(nt):
                        for k, a in enumerate(parts):
                            ins = mm(o[:, g * nt + t:g * nt + t + 1], a[:, t * P:t * P + P], ones[:, 0:1],
                                     start=(k == 0), stop=(k == len(parts) - 1))
                ins.then_inc(small_full, 1)

            def spread(n):
                pe.wait_ge(diag_ready, tl["diag"].up())
                o = sbank()
                mm(o[:, 0:n], ones, diag[:, 0:n], start=True, stop=True).then_inc(small_full, 1)

            def prenorm(c0):
                pe.wait_ge(sq_ready, tl["sq"].up(DC))
                stats([[uT[:, k, c0:T] for k in range(DC)]], (T - c0) // P)
                spread(T - c0)

            def out_proj(src, c0, turns, nb, per, kc):
                with repeat(pe, turns, (gemm, nb * per), (w_t[0], 32 * nb // 2), (w_t[1], 32 * nb // 2)) as i:
                    for b in range(nb):
                        s = b % 2
                        pe.wait_ge(w_in[s], w_t[s].up(32))
                        w = wring[:, s, 0:kc * per * P].rearrange("p (k n) -> p k n", k=kc)
                        for j in range(per):
                            o = gbank()
                            for k in range(kc):
                                ins = mm(o[:, 0:T - c0], w[:, k, j * P:j * P + P], src[:, k, c0:T],
                                         start=(k == 0), stop=(k == kc - 1))
                            ins.then_inc(gemm_full, 1)

            def attention(items, ocount):
                items = list(items)

                def scores(it):
                    for q, k in zip(it["q"], it["k"]):
                        o = gbank()
                        nk = it["nk"]
                        if "bias" in it:
                            mm(o[:, 0:nk], q, k, start=True, stop=False)
                            ins = mm(o[:, 0:nk], flip, it["bias"], start=False, stop=True)
                        elif "na" in it:
                            mm(o[:, 0:nk], q, k, start=True, stop=False)
                            pe.wait_ge(bias_ready, tl["bias"].up())
                            ins = mm(o[:, CTX:T], flip, maskb[:, it["na"][1], :], start=False, stop=True)
                        else:
                            ins = mm(o[:, 0:nk], q, k, start=True, stop=True)
                        ins.then_inc(gemm_full, 1)

                def turn(i, it):
                    pe.wait_ge(probn_ready, tl["probn"].up())
                    o = sbank()
                    for kt in range(it["nk"] // P):
                        ins = nc.tensor.transpose(o[:, kt * P:kt * P + P], probn[:, i % 2, kt * P:kt * P + P], ident)
                    ins.then_inc(small_full, 1)

                def values(i, it):
                    if i % 4 == 0:
                        b, full, free = opsum.take()
                        obank[0] = psum[b]
                        if opsum.n > 2:
                            pe.wait_ge(o_taken, opsum.n - 2)
                    pe.wait_ge(probT_ready, tl["probT"].up())
                    r0, r1 = it["rows"]
                    for kt, v in enumerate(it["v"]):
                        ins = mm(obank[0][r0:r1, it["cols"]:it["cols"] + P], v, probT[:, i % 2, kt, :],
                                 start=(kt == 0), stop=(kt == len(it["v"]) - 1))
                    ins.then_inc(pv_done, 1)

                obank = [None]
                scores(items[0])
                for i, it in enumerate(items):
                    if i + 1 < len(items):
                        scores(items[i + 1])
                    turn(i, it)
                    if i:
                        values(i - 1, items[i - 1])
                values(len(items) - 1, items[-1])

            def hybrid(l):
                def step_v(k=1):
                    pe.wait_ge(v_hyb, tl["vh"].up(k))

                def step_a(k=1):
                    pe.wait_ge(a_act, tl["aa"].up(k))

                pe.wait_ge(sq_ready, tl["sq"].up(DC))
                stats([[uT[:, k, CTX:T] for k in range(DC)]], 2)
                spread(SEQ)
                step_v()
                x = uT[:, :, CTX:T]
                for n, (c0, width) in enumerate(HY):
                    s = (19 * l + n) % 2
                    pe.wait_ge(w_in[s], w_t[s].up(32))
                    w = wring[:, s, 0:DC * width].rearrange("p (k n) -> p k n", k=DC)
                    if n == 11:
                        o = gbank()
                        for t in range(2):
                            for k in range(DC):
                                ins = mm(o[:, t * 8:t * 8 + 8], x[:, k, t * P:t * P + P], w[:, k, 0:8],
                                         start=(k == 0), stop=(k == DC - 1))
                        ins.then_inc(gemm_full, 1)
                    o = gbank()
                    if n == 13:
                        for t in range(2):
                            for k in range(DC):
                                ins = mm(o[:, t * 256:t * 256 + 256], x[:, k, t * P:t * P + P], w[:, k, :],
                                         start=(k == 0), stop=(k == DC - 1))
                    else:
                        cols = {1: [(0, P), (64, 160)], 11: [(8, 136), (136, 264)]}.get(n, [(0, P), (P, 2 * P)])
                        for j, (a, b) in enumerate(cols):
                            for k in range(DC):
                                ins = mm(o[0:b - a, j * SEQ:j * SEQ + SEQ], w[:, k, a:b], x[:, k, :],
                                         start=(k == 0), stop=(k == DC - 1))
                    ins.then_inc(gemm_full, 1)
                step_a()
                o = sbank()
                for t in range(2):
                    for k in range(2):
                        mm(o[:, t:t + 1], half[:, 0, k * SEQ + t * P:k * SEQ + t * P + P], ones[:, 0:1],
                           start=(k == 0), stop=(k == 1))
                for t in range(2):
                    ins = mm(o[:, 2 + t:3 + t], half[:, 1, t * P:t * P + P], ones[:, 0:1], start=True, stop=True)
                ins.then_inc(small_full, 1)
                spread(SEQ)
                spread(SEQ)
                step_v(2)
                if l == 0:
                    pass
                for p in range(2):
                    o = gbank()
                    for j in range(2):
                        h = 2 * p + j
                        for k in range(2):
                            ins = mm(o[0:MLA_QK, j * SEQ:j * SEQ + SEQ], wuq[:, l, k, h * MLA_QK:(h + 1) * MLA_QK],
                                     cq[:, k, :], start=(k == 0), stop=(k == 1))
                    ins.then_inc(gemm_full, 1)
                for p in range(2):
                    o = gbank()
                    for j in range(2):
                        h = 2 * p + j
                        ins = mm(o[0:NOPE, j * SEQ:j * SEQ + SEQ], wukv[:, l, h * P:h * P + NOPE], ckv,
                                 start=True, stop=True)
                    ins.then_inc(gemm_full, 1)
                for t in range(2):
                    o = gbank()
                    mm(o[:, :], ckv[:, t * P:t * P + P], wukv[:, l, :], start=True, stop=True).then_inc(gemm_full, 1)
                for p in range(2):
                    step_a()
                    o = sbank()
                    mm(o[0:MLA_QK, :], c("rot96")[0:MLA_QK, :], mq[0:MLA_QK, 2 * p:2 * p + 2, :],
                       start=True, stop=True).then_inc(small_full, 1)
                step_a(2)
                o = sbank()
                mm(o[0:MLA_QK, 0:SEQ], c("rot96")[0:MLA_QK, :], mk[0:MLA_QK, 0, :], start=True,
                   stop=True).then_inc(small_full, 1)
                step_v(5)
                if l == 0:
                    pe.wait_ge(brev_in, 16)
                attention([*mla_items(), *moba_items()], 4)
                step_a(3)
                step_a()
                stats([[uT[:, g, 0:SEQ]] for g in range(8)], 2)
                for p in range(4):
                    spread(T)
                step_v(3 + 4)
                for src in (4, 8):
                    for t in range(2):
                        o = gbank()
                        for h in range(GH):
                            ins = nc.tensor.transpose(o[:, h * P:h * P + P], cvo[:, src + h, t * P:t * P + P], ident)
                        ins.then_inc(gemm_full, 1)
                step_v(2)
                o = sbank()
                mm(o[:, 0:GN], upto, gs[:, 9, :], start=True, stop=True).then_inc(small_full, 1)
                for t in range(2):
                    o = gbank()
                    for h in range(GH):
                        ins = mm(o[:, h * P:h * P + P], gB[:, 4 * t + h, :], upto, start=True, stop=True)
                    ins.then_inc(gemm_full, 1)
                for first in (4, 0):
                    for t in range(2):
                        o = gbank()
                        for h in range(GH):
                            ins = mm(o[:, h * P:h * P + P], cvo[:, 4 + h, t * P:t * P + P],
                                     cvo[:, first + h, t * P:t * P + P], start=True, stop=True)
                        ins.then_inc(gemm_full, 1)
                step_v(2)
                for t in range(2):
                    o = gbank()
                    for h in range(GH):
                        ins = nc.tensor.transpose(o[:, h * P:h * P + P], LT[:, 4 * t + h, :], ident)
                    ins.then_inc(gemm_full, 1)
                step_v()
                for t in range(2):
                    o = gbank()
                    for h in range(GH):
                        ins = nc.tensor.transpose(o[:, h * P:h * P + P], Ym[:, 4 * t + h, :], ident)
                    ins.then_inc(gemm_full, 1)
                step_a(5)
                for m in range(1, LEVELS):
                    step_v()
                    for t in range(2):
                        o = gbank()
                        for h in range(GH):
                            n = 4 * t + h
                            ins = mm(o[:, h * P:h * P + P], LmT[:, n, :], Xm[:, n, :], start=True, stop=True)
                        ins.then_inc(gemm_full, 1)
                    for t in range(2):
                        step_a()
                        for which in range(2):
                            if which == 0 and m == LEVELS - 1:
                                continue
                            o = gbank()
                            for h in range(GH):
                                n = 4 * t + h
                                ins = mm(o[:, h * P:h * P + P], *((XT[:, n, :], Ym[:, n, :]) if which == 0 else
                                                                 (Ym[:, n, :], XT[:, n, :])), start=True, stop=True)
                            ins.then_inc(gemm_full, 1)
                step_v()

                def tiles(f):
                    o = gbank()
                    for h in range(GH):
                        pairs = f(h)
                        for k, (a, b) in enumerate(pairs):
                            ins = mm(o[:, h * P:h * P + P], a, b, start=(k == 0), stop=(k == len(pairs) - 1))
                    ins.then_inc(gemm_full, 1)

                tiles(lambda h: [(XT[:, h, :], vtk[:, h, :])])
                step_a()
                tiles(lambda h: [(ktok[:, h, :], Um[:, h, :])])
                tiles(lambda h: [(Um[:, h, :], ATm[:, h, :])])
                step_a()
                tiles(lambda h: [(cvo[:, 4 + h, P:2 * P], S1[:, h, :])])
                step_v()
                tiles(lambda h: [(XT[:, 4 + h, :], Rm[:, 4 + h, :])])
                step_a(2)
                tiles(lambda h: [(S1[:, h, :], qg[:, h, :]), (Um[:, 4 + h, :], ATm[:, 4 + h, :])])
                step_a()
                stats([[uT[:, g, 0:SEQ]] for g in range(4)], 2)
                for p in range(2):
                    spread(T)
                step_v()
                for b in range(4):
                    s = (19 * l + len(HY) + b) % 2
                    pe.wait_ge(w_in[s], w_t[s].up(32))
                    w = wring[:, s, 0:DC * 256].rearrange("p (k n) -> p k n", k=DC)
                    o = gbank()
                    for j in range(2):
                        for k in range(DC):
                            ins = mm(o[:, j * SEQ:j * SEQ + SEQ], w[:, k, j * P:j * P + P], yc[:, k, :],
                                     start=(k == 0), stop=(k == DC - 1))
                    ins.then_inc(gemm_full, 1)

            tl["g"].up(2)
            pe.wait_ge(const_in, 16)
            pe.wait_ge(vec_in, 16 * 12)
            o = sbank()
            for j, r in enumerate((128, 89, 72, 96)):
                ins = nc.tensor.transpose(o[:, j * P:j * P + r], vraw[0:r, j, :], ident[0:r, 0:r])
            ins.then_inc(small_full, 1)
            pe.wait_ge(x_in, 32)
            for k in range(DC):
                o = gbank()
                for t in range(TT):
                    ins = nc.tensor.transpose(o[:, t * P:t * P + P], stage[:, t, k * P:k * P + P], ident)
                ins.then_inc(gemm_full, 1)
            pe.wait_ge(misc_in, 16 * 9)
            pe.wait_ge(t5_set, 1)
            o = sbank()
            mm(o[0:5, 0:TAB], t5w[:, :], c("hot")[0:33, :], start=True, stop=True).then_inc(small_full, 1)
            pe.wait_ge(sc_ready, 1)
            for l in range(LAYERS):
                with pe.Fori(0, 6) as i:
                    for s in range(3):
                        pe.wait_ge(ada_in[s], i * 16 + (6 * l + 1) * 16)
                        for j in range(4):
                            for k in range(DC):
                                ins = mm(psum[7 - l][:, bass.ds(i * 24 + (s * 4 + j) * 2, 2)],
                                         adaw[:, s, k, j * P:j * P + P], sc[:, k, :], start=(k == 0), stop=(k == DC - 1))
                        ins.then_inc(ada_done, 1)

            for st in run:
                c0, streams = shape_of(st)
                if st.startswith("ffn"):
                    prenorm(c0)
                    pe.wait_ge(u_ready, tl["u"].up(DC * len(streams)))
                    with repeat(pe, FC // 2, (gemm, 4), (w_t[0], 32), (w_t[1], 32)) as i:
                        for s in range(2):
                            pe.wait_ge(w_in[s], w_t[s].up(32))
                            w = wring[:, s, 0:DC * 2 * P].rearrange("p (k n) -> p k n", k=DC)
                            for a in range(2):
                                o = gbank()
                                for k in range(DC):
                                    ins = mm(o[:, 0:T - c0], w[:, k, a * P:a * P + P], uT[:, k, c0:T],
                                             start=(k == 0), stop=(k == DC - 1))
                                ins.then_inc(gemm_full, 1)
                    pe.wait_ge(g_ready, tl["g"].up(FC))
                    out_proj(bigc, c0, 2, 4, 1, FC)
                    pe.wait_ge(sq_ready, tl["sq"].up(DC))
                    stats([[uT[:, k, c0:T] for k in range(DC)]], (T - c0) // P)
                    spread(T - c0)
                elif st in ("da", "na"):
                    prenorm(0)
                    pe.wait_ge(u_ready, tl["u"].up(DC * 2))
                    for q0 in (c0, 0):
                        with repeat(pe, 2, (gemm, 4), (w_t[0], 32), (w_t[1], 32)) as i:
                            for s in range(2):
                                pe.wait_ge(w_in[s], w_t[s].up(32))
                                w = wring[:, s, 0:DC * 256].rearrange("p (k n) -> p k n", k=DC)
                                for j in range(2):
                                    o = gbank()
                                    for k in range(DC):
                                        ins = mm(o[:, 0:T - q0], w[:, k, j * P:j * P + P], uT[:, k, q0:T],
                                                 start=(k == 0), stop=(k == DC - 1))
                                    ins.then_inc(gemm_full, 1)
                    pe.wait_ge(qkv_ready, tl["qkv"].up(16))
                    more = [(small, 8)] if st == "da" else []
                    with repeat(pe, 2, (gemm, 8), (w_t[0], 32), (w_t[1], 32), *more) as i:
                        for s in range(2):
                            pe.wait_ge(w_in[s], w_t[s].up(32))
                            w = wring[:, s, 0:DC * 256].rearrange("p (k n) -> p k n", k=DC)
                            for t in range(TT):
                                o = gbank()
                                for k in range(DC):
                                    ins = mm(o[:, 0:256], uT[:, k, t * P:t * P + P], w[:, k, :],
                                             start=(k == 0), stop=(k == DC - 1))
                                ins.then_inc(gemm_full, 1)
                                if st == "da":
                                    o = sbank()
                                    mm(o[:, 0:SEQ], c("rot"), bigc[:, bass.ds(i * 8 + s * 4 + t, 1), CTX:T],
                                       start=True, stop=True).then_inc(small_full, 1)
                    pe.wait_ge(v_ready, tl["v"].up(16))
                    if st == "da":
                        pe.wait_ge(rope_ready, 16)
                    attention(da_items() if st == "da" else na_items(), 4)
                    if st == "da":
                        pe.wait_ge(sq_ready, tl["sq"].up(8))
                        stats([[uT[:, h, :]] for h in range(8)], TT)
                        for h in range(8):
                            spread(T)
                    pe.wait_ge(on_ready, tl["on"].up(8))
                    out_proj(bigc, c0, 2, 2, 2, DC)
                    pe.wait_ge(sq_ready, tl["sq"].up(DC))
                    stats([[uT[:, k, c0:T] for k in range(DC)]], (T - c0) // P)
                    spread(T - c0)
                elif st.startswith("hy"):
                    hybrid(int(st[2]))
            if stop is None:
                pe.wait_ge(sq_ready, tl["sq"].up(DC))
                stats([[uT[:, k, CTX:T] for k in range(DC)]], 2)
                spread(SEQ)
                pe.wait_ge(v_hyb, tl["vh"].up())
                for t in range(2):
                    for g in range(2):
                        o = gbank()
                        for j in range(4):
                            ins = nc.tensor.transpose(o[:, j * P:j * P + P],
                                                      uT[:, 4 * g + j, CTX + t * P:CTX + t * P + P], ident)
                        ins.then_inc(gemm_full, 1)

        @block.scalar
        def _(act):
            gemm, small = Banks(0, 4), Banks(4, 2)
            own = Tally()
            tl = {k: Tally() for k in ("h", "var", "n", "g", "sq", "negm", "probn", "pv", "o", "vh", "aa")}

            def do(ins, *signals):
                ins.then_inc(act_step, 1)
                act.wait_ge(act_step, own.up())
                for s in signals:
                    act.sem_inc(s, 1)

            A_ = nc.scalar.activation

            def product(pool=None):
                pool = pool or gemm
                b, full, _ = pool.take()
                act.wait_ge(gemm_full if pool is gemm else small_full, full)
                return psum[b], (gemm_free if pool is gemm else small_free)[b - pool.first]

            def root(n):
                act.wait_ge(var_ready, tl["var"].up())
                do(A_(stat[:, 0, 0:n], stat[:, 0, 0:n], ACT.Sqrt), root_ready)

            def squares(c0):
                for k in range(DC):
                    act.wait_ge(h_ready, tl["h"].up())
                    do(A_(uT[:, k, c0:T], hT[:, k, c0:T], ACT.Square), sq_ready)

            def shift(l, sub, streams):
                for k in range(DC):
                    for s in streams:
                        act.wait_ge(n_ready, tl["n"].up())
                        u = uT[:, k, s * CTX:s * CTX + SEQ]
                        do(A_(u, u, ACT.Identity, bias=mod[:, l, 3 * sub * DC + k, s:s + 1]), u_ready)

            def outputs(c0, turns, per):
                with repeat(act, turns, (gemm, per), (own, 2 * per)) as i:
                    for j in range(per):
                        o, free = product()
                        k = bass.ds(i * per + j, 1)
                        do(A_(yT[:, k, c0:T], o[:, 0:T - c0].rearrange("p (a n) -> p a n", a=1), ACT.Copy))
                        do(A_(uT[:, k, c0:T], o[:, 0:T - c0].rearrange("p (a n) -> p a n", a=1), ACT.Square),
                           free, sq_ready)

            def attention(items):
                items = list(items)

                def exps(i, it):
                    act.wait_ge(negm_ready, tl["negm"].up())
                    if i >= 2:
                        act.wait_ge(probn_ready, tl["probn"].now() + i - 1)
                    for j in range(len(it["q"])):
                        o, free = product()
                        do(A_(prob[:, i % 2, j, 0:it["nk"]], o[:, 0:it["nk"]], ACT.Exp, bias=negm[:, i % 2, 1, j:j + 1],
                              scale=it["scale"], accum_out=rsum[:, i % 2, 0, j:j + 1]), free)
                    act.sem_inc(exp_ready, 1)

                def turned(i, it):
                    o, free = product(small)
                    if i >= 2:
                        act.wait_ge(pv_done, tl["pv"].now() + i - 1)
                    nk = it["nk"]
                    do(A_(probT[:, i % 2, 0:nk // P, :], o[:, 0:nk].rearrange("p (a n) -> p a n", n=P), ACT.Copy),
                       free, probT_ready)

                exps(0, items[0])
                for i, it in enumerate(items):
                    if i + 1 < len(items):
                        exps(i + 1, items[i + 1])
                    turned(i, it)
                tl["probn"].up(len(items))
                tl["pv"].up(len(items))

            def skip_small(n):
                small.up(n)

            def hybrid(l):
                def step_v(k=1):
                    act.wait_ge(v_hyb, tl["vh"].up(k))

                squares(CTX)
                root(2)
                small.up(2)
                step_v()
                for n in range(15):
                    if n in (3, 4, 5, 6, 7, 8, 13):
                        gemm.up()
                        continue
                    if n == 11:
                        gemm.up()
                    o, free = product()
                    o3 = o[:, :].rearrange("p (a n) -> p a n", a=2)
                    if n == 0:
                        do(A_(cq, o3, ACT.Copy), free)
                    elif n == 1:
                        do(A_(ckv, o[:, 0:SEQ], ACT.Copy))
                        do(A_(mk[64:96, 0, :], o[64:96, SEQ:T], ACT.Copy), free)
                    elif n == 11:
                        do(A_(mbq, o3, ACT.Copy, scale=0.125), free)
                    elif n == 12:
                        do(A_(mbk, o3, ACT.Copy), free)
                    else:
                        dst = {2: mgate, 9: gz[:, 0:2, :], 10: gz[:, 2:4, :], 14: cgate}[n]
                        do(A_(dst, o3, ACT.Silu), free)
                do(A_(half[:, 0, :], cq, ACT.Square))
                do(A_(half[:, 1, 0:SEQ], ckv, ACT.Square), a_act)
                root(4)
                small.up(3)
                step_v(2)
                for p in range(2):
                    o, free = product()
                    do(A_(mq[0:MLA_QK, 2 * p:2 * p + 2, :], o[0:MLA_QK, :].rearrange("p (a n) -> p a n", a=2), ACT.Copy,
                          scale=STEPS), free, a_act)
                for p in range(2):
                    o, free = product()
                    do(A_(mk[0:NOPE, 2 * p:2 * p + 2, :], o[0:NOPE, :].rearrange("p (a n) -> p a n", a=2), ACT.Copy),
                       free, a_act)
                gemm.up(2)
                small.up(3)
                step_v(5)
                attention([*mla_items(), *moba_items()])
                for g in range(3):
                    step_v()
                    do(A_(cvo[:, 4 * g:4 * g + 4, :], cvo[:, 4 * g:4 * g + 4, :], ACT.Silu), a_act)
                do(A_(uT[:, 0:8, 0:SEQ], cvo[:, 0:8, :], ACT.Square), a_act)
                root(16)
                small.up(5)
                step_v(4)
                for dst in (ktok, vtk):
                    for t in range(2):
                        o, free = product()
                        do(A_(dst[:, 4 * t:4 * t + 4, :], o[:, :].rearrange("p (a n) -> p a n", n=P), ACT.Copy), free)
                act.sem_inc(a_act, 1)
                step_v()
                do(A_(gs[:, 6, :], gs[:, 4, :], ACT.Exp))
                do(A_(gs[:, 7, :].rearrange("p (a n) -> p a n", a=2), gs[:, 0:2, 0:GH], ACT.Exp, scale=-1.0))
                do(A_(gs[:, 8, 0:GH], galog[:, l, 0, :], ACT.Exp))
                do(A_(gs[:, 6, :], gs[:, 6, :], ACT.Ln, bias=1.0), a_act)
                step_v()
                small.up()
                step_v()
                gemm.up()
                o, free = product()
                do(A_(EG, o[:, :].rearrange("p (a n) -> p a n", n=P), ACT.Exp), free)
                do(A_(DTm, DTm, ACT.Exp))
                do(A_(gs[:, 11, 0:GH], gs[:, 11, 0:GH], ACT.Exp))
                do(A_(gs[:, 12, :], gs[:, 10, :], ACT.Exp), a_act)
                gemm.up(4)
                step_v()
                gemm.up(2)
                step_v()
                for t in range(2):
                    o, free = product()
                    do(A_(LT[:, 4 * t:4 * t + 4, :], o[:, :].rearrange("p (a n) -> p a n", n=P), ACT.Copy), free, a_act)
                for m in range(1, LEVELS):
                    step_v()
                    for t in range(2):
                        o, free = product()
                        do(A_(Ym[:, 4 * t:4 * t + 4, :], o[:, :].rearrange("p (a n) -> p a n", n=P), ACT.Copy),
                           free, a_act)
                    gemm.up(2 if m == LEVELS - 1 else 4)
                step_v()

                def keep(dst):
                    o, free = product()
                    do(A_(dst, o[:, :].rearrange("p (a n) -> p a n", n=P), ACT.Copy), free, a_act)

                keep(Um[:, 0:4, :])
                keep(S1)
                keep(oraw[:, :, 0:P])
                gemm.up()
                step_v()
                keep(Um[:, 4:8, :])
                o, free = product()
                do(A_(oraw[:, :, P:2 * P], o[:, :].rearrange("p (a n) -> p a n", n=P), ACT.Copy), free)
                do(A_(uT[:, 0:4, 0:SEQ], oraw, ACT.Square), a_act)
                root(8)
                small.up(3)
                step_v()
                gemm.up(4)

            tl["g"].up()
            act.wait_ge(vec_ready, 1)
            do(A_(sc[:, :, 0], vec[:, 0, V_CC:V_CC + DC], ACT.Silu))
            do(A_(sc[:, :, 1], vec[:, 0, V_C:V_C + DC], ACT.Silu), sc_ready)
            small.up(2)
            gemm.up(DC)
            act.wait_ge(lam_exp, 1)
            do(A_(lams[:, 2:4], lams[:, 0:2], ACT.Exp), lam_exp)

            for st in run:
                c0, streams = shape_of(st)
                if st in SUB:
                    l, sub = SUB[st]
                    squares(0 if st == "na" else c0)
                    root(TT if st == "na" else (T - c0) // P)
                    small.up(2)
                    shift(l, sub, [0, 1] if st == "na" else streams)
                if st.startswith("ffn"):
                    with repeat(act, FC // 2, (gemm, 4), (own, 2), (tl["g"], 2)) as i:
                        for s in range(2):
                            o, _ = product()
                            act.wait_ge(g_ready, tl["g"].now())
                            tl["g"].up()
                            do(A_(half[:, s, 0:T - c0], o[:, 0:T - c0], ACT.Silu), silu_ready)
                            gemm.up()
                    outputs(c0, 2, 4)
                    root((T - c0) // P)
                    small.up(2)
                elif st in ("da", "na"):
                    for which, q0 in enumerate((c0, 0)):
                        with repeat(act, 2, (gemm, 4), (own, 4)) as i:
                            for j in range(4):
                                o, free = product()
                                do(A_(bigc[:, bass.ds(i * 4 + (8 * which + j), 1), q0:T],
                                      o[:, 0:T - q0].rearrange("p (a n) -> p a n", a=1), ACT.Copy,
                                      scale=0.125 if st == "na" and which == 0 else 1.0), free, qkv_ready)
                    gemm.up(16)
                    if st == "da":
                        small.up(16)
                    attention(da_items() if st == "da" else na_items())
                    if st == "da":
                        for h in range(8):
                            act.wait_ge(o_ready, h + 1)
                            do(A_(uT[:, h, :], bigc[:, h, :], ACT.Square), sq_ready)
                        root(8 * TT)
                        small.up(9)
                    outputs(c0, 2, 4)
                    root((T - c0) // P)
                    small.up(2)
                elif st.startswith("hy"):
                    hybrid(int(st[2]))
            if stop is None:
                squares(CTX)
                root(2)
                small.up(2)
                for t in range(2):
                    for g in range(2):
                        o, free = product()
                        do(A_(stage[:, t, g * 512:(g + 1) * 512], o[:, :], ACT.Copy), free)
            act.sem_inc(out_ready, 1)

        @block.vector
        def _(dve):
            gemm, small = Banks(0, 4), Banks(4, 2)
            own = Tally()
            tl = {k: Tally() for k in ("root", "silu", "exp", "pv", "aa")}
            V = nc.vector

            def do(ins, *signals):
                ins.then_inc(vec_step, 1)
                dve.wait_ge(vec_step, own.up())
                for s in signals:
                    dve.sem_inc(s, 1)

            def product(pool=None):
                pool = pool or gemm
                b, full, _ = pool.take()
                dve.wait_ge(gemm_full if pool is gemm else small_full, full)
                return psum[b], (gemm_free if pool is gemm else small_free)[b - pool.first]

            def norm_stats(n, means):
                o, free = product(small)
                for a, b, inv, eps in means:
                    do(V.tensor_scalar(stat[:, 0, a:b], o[:, a:b], inv, eps, ALU.mult, ALU.add))
                dve.sem_inc(free, 1)
                dve.sem_inc(var_ready, 1)
                dve.wait_ge(root_ready, tl["root"].up())
                do(V.reciprocal(stat[:, 1, 0:n], stat[:, 0, 0:n]))

            def spread(a, nt):
                do(V.tensor_tensor(diag[:, 0:nt * P].rearrange("p (a n) -> p a n", n=P), rep(ident, nt),
                                   wide(stat[:, 1, a:a + nt], P), ALU.mult), diag_ready)
                return product(small)

            def stt(out_, in0, scalar, in1, op0=ALU.mult, op1=ALU.mult):
                return V.scalar_tensor_tensor(out=out_, in0=in0, scalar=scalar, in1=in1, op0=op0, op1=op1)

            def prenorm(i6, c0, streams):
                nt = (T - c0) // P
                norm_stats(nt, [(0, nt, 1.0 / D, EPS)])
                r, free = spread(0, nt)
                for k in range(DC):
                    for s in streams:
                        a = s * CTX
                        do(stt(uT[:, k, a:a + SEQ], hT[:, k, a:a + SEQ], coefA[:, i6, k, s:s + 1],
                               r[:, a - c0:a - c0 + SEQ]), n_ready)
                dve.sem_inc(free, 1)

            def residual(i6, c0, streams):
                nt = (T - c0) // P
                norm_stats(nt, [(0, nt, 1.0 / D, EPS)])
                r, free = spread(0, nt)
                for k in range(DC):
                    for s in streams:
                        a = s * CTX
                        do(stt(yT[:, k, a:a + SEQ], yT[:, k, a:a + SEQ], coefG[:, i6, k, s:s + 1],
                               r[:, a - c0:a - c0 + SEQ]))
                    do(V.tensor_tensor(hT[:, k, c0:T], hT[:, k, c0:T], yT[:, k, c0:T], ALU.add), h_ready)
                dve.sem_inc(free, 1)

            def attention(items, take):
                items = list(items)

                def table(i, it):
                    h, t = it["na"]
                    if i >= 2:
                        dve.wait_ge(gemm_full, gemm.n)
                    m = maskb[:, t, :].rearrange("p (r n) -> p r n", r=ROWS)
                    raw = rawb[:, t, h, 0:1]
                    raw = bass.AP(tensor=raw.tensor, offset=raw.offset, ap=[raw.ap[0], [RPB_C, ROWS], [1, GRID_W]])
                    do(V.tensor_tensor(m, raw, rep(c("win"), ROWS), ALU.mult))
                    do(V.tensor_tensor(m, m, rep(c("notwin"), ROWS), ALU.add), bias_ready)

                def peak(i, it):
                    for j in range(len(it["q"])):
                        o, _ = product()
                        do(V.reduce_max(negm[:, i % 2, 0, j:j + 1], o[:, 0:it["nk"]], AX.X))
                    n = len(it["q"])
                    do(V.tensor_scalar(negm[:, i % 2, 1, 0:n], negm[:, i % 2, 0, 0:n], -it["scale"], None, ALU.mult),
                       negm_ready)

                def normalise(i, it):
                    n, nk, b = len(it["q"]), it["nk"], i % 2
                    dve.wait_ge(exp_ready, tl["exp"].up())
                    do(V.reciprocal(rsum[:, b, 1, 0:n], rsum[:, b, 0, 0:n]))
                    if i >= 2:
                        dve.wait_ge(small_full, small.n + i - 1)
                    if n == 2:
                        do(V.tensor_scalar(lams[:, 5:6], rsum[:, b, 1, 1:2], lams[:, 4:5], None, ALU.mult))
                        do(V.tensor_scalar(prob[:, b, 1, 0:nk], prob[:, b, 1, 0:nk], lams[:, 5:6], None, ALU.mult))
                        do(stt(probn[:, b, 0:nk], prob[:, b, 0, 0:nk], rsum[:, b, 1, 0:1], prob[:, b, 1, 0:nk],
                               ALU.mult, ALU.add), probn_ready)
                    else:
                        do(V.tensor_scalar(probn[:, b, 0:nk], prob[:, b, 0, 0:nk], rsum[:, b, 1, 0:1], None, ALU.mult),
                           probn_ready)

                def output(i):
                    if i % 4 == 3:
                        dve.wait_ge(pv_done, tl["pv"].now() + i + 1)
                        take(i // 4, psum[6 + obank[0] % 2])
                        obank[0] += 1

                if "na" in items[0]:
                    table(0, items[0])
                    table(1, items[1])
                peak(0, items[0])
                for i, it in enumerate(items):
                    if i + 2 < len(items) and "na" in it:
                        table(i + 2, items[i + 2])
                    if i + 1 < len(items):
                        peak(i + 1, items[i + 1])
                    normalise(i, it)
                    if i:
                        output(i - 1)
                output(len(items) - 1)
                small.up(len(items))
                tl["pv"].up(len(items))

            obank = [0]

            def hybrid(l):
                def step_a(k=1):
                    dve.wait_ge(a_act, tl["aa"].up(k))

                norm_stats(2, [(0, 2, 1.0 / D, EPS)])
                r, free = spread(0, 2)
                for k in range(DC):
                    do(stt(uT[:, k, CTX:T], hT[:, k, CTX:T], vec[:, 0, V_NW + l * DC + k:V_NW + l * DC + k + 1],
                           r[:, 0:SEQ]))
                dve.sem_inc(free, 1)
                dve.sem_inc(v_hyb, 1)
                do(V.memset(convin[:, :, 0:PAD], 0.0))
                for n in range(15):
                    if 3 <= n <= 8:
                        o, free = product()
                        do(V.tensor_copy(convin[:, 2 * (n - 3):2 * (n - 3) + 2, PAD:PAD + SEQ],
                                         o[:, :].rearrange("p (a n) -> p a n", a=2)), free)
                    elif n == 11:
                        o, free = product()
                        do(V.tensor_copy(gs[:, 0:2, :], o[:, 0:16].rearrange("p (a n) -> p a n", a=2)), free)
                        gemm.up()
                    elif n == 13:
                        o, free = product()
                        do(V.tensor_copy(mbv, o[:, :].rearrange("p (a n) -> p a n", a=2)), free)
                    else:
                        gemm.up()
                step_a()
                norm_stats(4, [(0, 2, 1.0 / 256, EPS), (2, 4, 1.0 / 128, EPS)])
                r, free = spread(0, 2)
                for k in range(2):
                    do(stt(cq[:, k, :], cq[:, k, :], vec[:, 1, V_Q + 2 * l + k:V_Q + 2 * l + k + 1], r[:, 0:SEQ]))
                dve.sem_inc(free, 1)
                dve.sem_inc(v_hyb, 1)
                r, free = spread(2, 2)
                do(stt(ckv, ckv, vec[:, 1, V_KV + l:V_KV + l + 1], r[:, 0:SEQ]), free, v_hyb)
                step_a(4)
                gemm.up(4)
                for t in range(2):
                    o, free = product()
                    do(V.tensor_copy(mv[:, t, :].rearrange("p (h n) -> p h n", h=4),
                                     o[:, :].rearrange("p (h n) -> p h n", h=4)[:, :, NOPE:P]), free, v_hyb)
                for p in range(2):
                    o, free = product(small)
                    x = mq[0:MLA_QK, 2 * p:2 * p + 2, :]
                    tmp = half[0:MLA_QK, 0, :].rearrange("p (a n) -> p a n", a=2)
                    do(V.tensor_tensor(tmp, o[0:MLA_QK, :].rearrange("p (a n) -> p a n", a=2),
                                       rep(c("sin96")[0:MLA_QK, :], 2), ALU.mult), free)
                    do(V.tensor_tensor(x, x, rep(c("cos96")[0:MLA_QK, :], 2), ALU.mult))
                    do(V.tensor_tensor(x, x, tmp, ALU.add), v_hyb)
                o, free = product(small)
                do(V.tensor_tensor(half[64:96, 0, 0:SEQ], o[64:96, 0:SEQ], c("sin96")[64:96, :], ALU.mult), free)
                do(V.tensor_tensor(half[64:96, 1, 0:SEQ], mk[64:96, 0, :], c("cos96")[64:96, :], ALU.mult))
                do(V.tensor_tensor(mk[64:96, :, :], rep(half[64:96, 0, 0:SEQ], 4), rep(half[64:96, 1, 0:SEQ], 4),
                                   ALU.add), v_hyb)

                def take(k, o):
                    gate = (mgate if k < 2 else cgate)[:, k % 2, :]
                    do(V.tensor_tensor(yc[:, (0, 1, 6, 7)[k], :], o[:, 0:SEQ], gate, ALU.mult), o_taken)

                attention([*mla_items(), *moba_items()], take)
                for k in range(12):
                    for j in range(CONV):
                        w = vec[:, 3, (l * CONV + j) * 12 + k:(l * CONV + j) * 12 + k + 1]
                        x = convin[:, k, j:j + SEQ]
                        if j == 0:
                            do(V.tensor_scalar(cvo[:, k, :], x, w, None, ALU.mult))
                        else:
                            do(stt(cvo[:, k, :], x, w, cvo[:, k, :], ALU.mult, ALU.add))
                    if k % 4 == 3:
                        dve.sem_inc(v_hyb, 1)
                step_a(4)
                norm_stats(16, [(0, 16, 1.0, EPS)])
                for p in range(4):
                    r, free = spread(4 * p, 4)
                    x = cvo[:, 2 * p:2 * p + 2, :]
                    do(stt(x, x, P ** -0.5 if p < 2 else 1.0, r[:, :].rearrange("p (a n) -> p a n", a=2)), free, v_hyb)
                gemm.up(4)
                ab = gs[:, 0:2, GH:2 * GH]

                def g2(j):
                    return gs[:, j, :].rearrange("p (a n) -> p a n", a=2)

                do(V.tensor_tensor(g2(3), ab, rep(galog[:, l, 1, :], 2), ALU.add))
                do(V.tensor_scalar(gs[:, 4, :], gs[:, 3, :], -1.0, None, ALU.mult))
                do(V.tensor_scalar(gs[:, 5, :], gs[:, 3, :], 0.0, None, ALU.max))
                do(V.tensor_tensor(gs[:, 4, :], gs[:, 3, :], gs[:, 4, :], ALU.min), v_hyb)
                step_a(2)
                do(V.tensor_tensor(gs[:, 5, :], gs[:, 5, :], gs[:, 6, :], ALU.add))
                do(stt(g2(9), g2(5), -1.0, rep(gs[:, 8, 0:GH], 2)))
                do(V.tensor_scalar(gs[:, 7, :], gs[:, 7, :], 1.0, None, ALU.add))
                do(V.reciprocal(gs[:, 2, :], gs[:, 7, :]))
                do(V.tensor_copy(gB, wide(gs[:, 9, :], P)), v_hyb)
                o, free = product(small)
                do(V.tensor_copy(gs[:, 10, :], o[:, 0:GN]), free)
                for t in range(2):
                    o, free = product()
                    for h in range(GH):
                        n = 4 * t + h
                        do(stt(DTm[:, n, :], o[:, h * P:h * P + P], gs[:, 10, n:n + 1], c("future"), ALU.subtract,
                               ALU.add))
                    if t == 0:
                        do(V.tensor_tensor(gs[:, 11, 0:GH], o[:, :].rearrange("p (a n) -> p a n", n=P)[:, :, P - 1],
                                           gs[:, 10, 0:GH], ALU.subtract), free)
                dve.sem_inc(v_hyb, 1)
                step_a()
                do(stt(gs[:, 13, :], gs[:, 2, :], -1.0, gs[:, 12, :]))
                do(V.tensor_tensor(qg, EG, cvo[:, 0:GH, P:2 * P], ALU.mult))
                do(V.tensor_tensor(ktok[:, 0:GH, :], ktok[:, 0:GH, :], wide(gs[:, 11, 0:GH], P), ALU.mult))
                do(V.tensor_tensor(vtk, vtk, wide(gs[:, 2, :], P), ALU.mult))
                for t in range(2):
                    o, free = product()
                    x = LT[:, 4 * t:4 * t + 4, :]
                    do(V.tensor_tensor(x, o[:, :].rearrange("p (a n) -> p a n", n=P), DTm[:, 4 * t:4 * t + 4, :],
                                       ALU.mult), free)
                    do(V.tensor_tensor(x, x, rep(c("strict"), 4), ALU.mult))
                dve.sem_inc(v_hyb, 1)
                for t in range(2):
                    o, free = product()
                    do(V.tensor_tensor(ATm[:, 4 * t:4 * t + 4, :], o[:, :].rearrange("p (a n) -> p a n", n=P),
                                       DTm[:, 4 * t:4 * t + 4, :], ALU.mult), free)
                for t in range(2):
                    o, free = product()
                    do(V.tensor_tensor(Ym[:, 4 * t:4 * t + 4, :], o[:, :].rearrange("p (a n) -> p a n", n=P),
                                       wide(gs[:, 2, 4 * t:4 * t + 4], P), ALU.mult), free)
                dve.sem_inc(v_hyb, 1)
                do(V.tensor_tensor(Xm, Ym, rep(c("low0"), GN), ALU.mult))
                do(stt(Xm, Xm, -1.0, rep(ident, GN), ALU.mult, ALU.add))
                gemm.up(2)
                step_a(2)

                def level(m):
                    a = CONST_COLS["lowT"][0] + m * P
                    return rep(cst[:, a:a + P], GN)

                do(V.tensor_tensor(XT, LT, level(0), ALU.mult))
                do(stt(XT, XT, -1.0, rep(ident, GN), ALU.mult, ALU.add))
                for m in range(1, LEVELS):
                    do(V.tensor_tensor(LmT, LT, level(m), ALU.mult), v_hyb)
                    gemm.up(2)
                    step_a(2)
                    for t in range(2):
                        for which in range(2):
                            if which == 0 and m == LEVELS - 1:
                                continue
                            o, free = product()
                            x = (XT if which else Xm)[:, 4 * t:4 * t + 4, :]
                            do(V.tensor_tensor(x, x, o[:, :].rearrange("p (a n) -> p a n", n=P), ALU.subtract), free)
                dve.sem_inc(v_hyb, 1)
                gemm.up(3)
                step_a(3)
                o, free = product()
                x = Rm[:, 4:8, :]
                do(V.tensor_tensor(x, o[:, :].rearrange("p (a n) -> p a n", n=P), wide(gs[:, 13, 4:8], P), ALU.mult),
                   free)
                do(V.tensor_tensor(x, x, vtk[:, 4:8, :], ALU.add), v_hyb)
                gemm.up(2)
                step_a(2)
                norm_stats(8, [(0, 8, 1.0 / P, EPS)])
                for p in range(2):
                    r, free = spread(4 * p, 4)
                    x = oraw[:, 2 * p:2 * p + 2, :]
                    do(stt(x, x, vec[:, 1, V_GN + l:V_GN + l + 1], r[:, :].rearrange("p (a n) -> p a n", a=2)), free)
                    do(V.tensor_tensor(yc[:, 2 + 2 * p:4 + 2 * p, :], x, gz[:, 2 * p:2 * p + 2, :], ALU.mult))
                dve.sem_inc(v_hyb, 1)
                for b in range(4):
                    o, free = product()
                    x = hT[:, 2 * b:2 * b + 2, CTX:T]
                    do(V.tensor_tensor(x, x, o[:, :].rearrange("p (a n) -> p a n", a=2), ALU.add), free, h_ready,
                       h_ready)

            dve.sem_inc(g_ready, 2)
            do(V.memset(t5w[0:32, 4:5], 0.0))
            do(V.memset(t5w[32:33, :], 1.0), t5_set)
            o, free = product(small)
            for j, r in enumerate((128, 89, 72, 96)):
                do(V.tensor_copy(vec[:, j, 0:r], o[:, j * P:j * P + r]))
            dve.sem_inc(free, 1)
            dve.sem_inc(vec_ready, 1)
            for k in range(DC):
                o, free = product()
                do(V.tensor_copy(hT[:, k, :], o[:, :]), free, h_ready)
            o, free = product(small)
            do(V.tensor_copy(tline[:, :], o[0:5, 0:TAB]), free, line_ready)
            dve.wait_ge(lam_in, 16)
            for j in range(2):
                do(V.tensor_tensor_reduce(half[:, 0, 0:64], lamv[:, 128 * j:128 * j + 64],
                                          lamv[:, 128 * j + 64:128 * j + 128], 1.0, 0.0, ALU.mult, ALU.add,
                                          lams[:, j:j + 1]))
            dve.sem_inc(lam_exp, 1)
            dve.wait_ge(lam_exp, 2)
            do(V.tensor_tensor(lams[:, 4:5], lams[:, 3:4], lams[:, 2:3], ALU.subtract))
            do(V.tensor_scalar(lams[:, 4:5], lams[:, 4:5], -LAM_INIT, None, ALU.add))
            do(V.tensor_scalar(lams[:, 6:7], vec[:, 1, V_SUB:V_SUB + 1], 1.0 - LAM_INIT, None, ALU.mult))
            for l in range(LAYERS):
                dve.wait_ge(ada_done, 18 * (l + 1))
                do(V.tensor_tensor(mod[:, l], psum[7 - l][:, 0:2 * N_MOD * DC].rearrange("p (a n) -> p a n", n=2),
                                   wide(vec[:, 1 + l, 0:N_MOD * DC], 2), ALU.add))
                for sub in range(3):
                    i6 = 3 * l + sub
                    m = mod[:, l]
                    do(stt(coefA[:, i6], m[:, (3 * sub + 1) * DC:(3 * sub + 2) * DC, :], 1.0, wide(v_norm(l, 2 * sub), 2),
                           ALU.add, ALU.mult))
                    do(stt(coefG[:, i6], m[:, (3 * sub + 2) * DC:(3 * sub + 3) * DC, :], 1.0 if sub == 1 else 0.5,
                           wide(v_norm(l, 2 * sub + 1), 2)))

            for st in run:
                c0, streams = shape_of(st)
                if st in SUB:
                    l, sub = SUB[st]
                    both = st == "na"
                    prenorm(3 * l + sub, 0 if both else c0, [0, 1] if both else streams)
                if st.startswith("ffn"):
                    with repeat(dve, FC // 2, (gemm, 4), (own, 2), (tl["silu"], 2)) as i:
                        for s in range(2):
                            _, free_a = product()
                            o, free_b = product()
                            dve.wait_ge(silu_ready, tl["silu"].up())
                            do(V.tensor_tensor(bigc[:, bass.ds(i * 2 + s, 1), c0:T],
                                               half[:, s:s + 1, 0:T - c0],
                                               o[:, 0:T - c0].rearrange("p (a n) -> p a n", a=1), ALU.mult),
                               free_a, free_b, g_ready)
                    gemm.up(8)
                    residual(3 * l + sub, c0, streams)
                elif st in ("da", "na"):
                    gemm.up(16)
                    more = [(small, 8)] if st == "da" else []
                    with repeat(dve, 2, (gemm, 8), (own, 8 + (24 if st == "da" else 0)), *more) as i:
                        for s in range(2):
                            for t in range(TT):
                                o, free = product()
                                do(V.tensor_copy(vtok[:, t, bass.ds(i * 512 + s * 256, 256)], o[:, 0:256]), free, v_ready)
                                if st == "da":
                                    o, free = product(small)
                                    x = bigc[:, bass.ds(i * 8 + s * 4 + t, 1), CTX:T]
                                    one = "p (a n) -> p a n"
                                    do(V.tensor_tensor(half[:, 0, 0:SEQ], o[:, 0:SEQ], c("sin"), ALU.mult), free)
                                    do(V.tensor_tensor(x, x, c("cos").rearrange(one, a=1), ALU.mult))
                                    do(V.tensor_tensor(x, x, half[:, 0, 0:SEQ].rearrange(one, a=1), ALU.add), rope_ready)
                    if st == "da":
                        def take(k, o):
                            do(V.tensor_copy(bigc[:, k, :], o[:, :]), o_taken, o_ready)
                    else:
                        dve.wait_ge(rawb_in, 16 * 4)

                        def take(k, o):
                            do(V.tensor_copy(bigc[:, k, CTX:T], o[:, 0:SEQ]), o_taken, on_ready)
                    attention(da_items() if st == "da" else na_items(), take)
                    if st == "da":
                        norm_stats(32, [(0, 32, 1.0 / P, EPS)])
                        for h in range(8):
                            r, free = spread(4 * h, 4)
                            do(stt(bigc[:, h, :], bigc[:, h, :], lams[:, 6:7], r[:, :]), free, on_ready)
                    gemm.up(8)
                    residual(3 * l + sub, c0, streams)
                elif st.startswith("hy"):
                    hybrid(int(st[2]))
            if stop is None:
                norm_stats(2, [(0, 2, 1.0 / D, EPS)])
                r, free = spread(0, 2)
                for k in range(DC):
                    do(stt(uT[:, k, CTX:T], hT[:, k, CTX:T], vec[:, 1, V_FIN + k:V_FIN + k + 1], r[:, 0:SEQ]))
                dve.sem_inc(v_hyb, 1)
            else:
                dve.sem_inc(out_ready, 1)



INS = ["x", "c", "ctx", "c_ctx", "ada_w", "ada_b", "norm_g", "ffn_w_in", "ffn_w_out", "da_w_in", "da_w_out",
       "da_lambda", "da_subln_g", "na_w_in", "na_w_out", "na_rpb", "norm_w_2", "w_in_2", "mla_q_norm_2",
       "mla_w_uq_2", "mla_kv_norm_2", "mla_w_ukv_2", "gdn_conv_w_2", "gdn_A_log_2", "gdn_dt_bias_2",
       "gdn_norm_w_2", "w_out_2", "t5_table_2", "final_norm_w_2"]


def kernel(**inputs):
    import concourse.bacc as bacc
    from concourse.bass_utils import run_bass_kernel_spmd

    nc = bacc.Bacc("TRN2", target_bir_lowering=False, num_devices=1)
    arrays, A = {}, {}
    for name in INS:
        a = np.ascontiguousarray(inputs[name])
        arrays[f"in_{name}"] = a
        A[name] = nc.dram_tensor(f"in_{name}", a.shape, F32, kind="ExternalInput").ap()
    arrays["in_constants"] = CONSTS
    const = nc.dram_tensor("in_constants", CONSTS.shape, F32, kind="ExternalInput").ap()
    tab = nc.dram_tensor("distance_lines", (5, TAB), F32).ap()
    out = nc.dram_tensor("out_rows", (1, SEQ, D), F32, kind="ExternalOutput").ap()
    build(nc, A, out, const, tab)
    r = run_bass_kernel_spmd(nc, [arrays], core_ids=[0])
    return r.results[0]["out_rows"]
```

```python
from contextlib import ExitStack, contextmanager

import numpy as np

import concourse.bass as bass
from concourse import mybir

F32 = mybir.dt.float32
F32R = mybir.dt.float32r
ALU = mybir.AluOpType
ACT = mybir.ActivationFunctionType
AX = mybir.AxisListType

P = 128
D = 1024
DC = D // P
CTX, SEQ = 256, 256
T = CTX + SEQ
TT = T // P
LAYERS = 2
N_MOD = 9
F = 2816
FC = F // P
F0 = 12
SLOT = DC * 256
EPS = 1e-6
GRID_W = 64
ROWS = SEQ // GRID_W
NA_ROWS, NA_COLS = 8, 16
NA_H = 16
RPB_R, RPB_C = 2 * NA_ROWS - 1, 2 * NA_COLS - 1
SPAN = (ROWS - 1) * RPB_C + GRID_W
LAM_INIT = 0.2
NEG = -1e30
IN2 = 3752
MLA_H, NOPE, ROPE, MLA_QK = 4, 64, 32, 96
GH = 4
GN = GH * (SEQ // P)
LEVELS = 7
CONV = 4
TAB = 384
PAD = CONV - 1


CONST_COLS = {}


def _constants():
    f = np.float32
    i = np.arange(P)
    parts = {}
    parts["ident"] = np.eye(P, dtype=f)
    parts["flip"] = np.eye(P, dtype=f)[::-1]
    parts["ones"] = np.ones((P, P), f)
    parts["upto"] = (i[:, None] <= i[None, :]).astype(f)
    parts["future"] = np.where(i[None, :] >= i[:, None], 0.0, NEG).astype(f)
    parts["strict"] = (i[None, :] > i[:, None]).astype(f)
    low = []
    for m in range(LEVELS):
        b = 2 ** m
        tb, jb = i[:, None] // b, i[None, :] // b
        low.append(((tb // 2 == jb // 2) & (tb % 2 == 1) & (jb % 2 == 0)).astype(f))
    parts["low0"] = low[0]
    parts["lowT"] = np.concatenate([x.T for x in low], axis=1)
    d = np.arange(P)
    rot = np.zeros((P, P), f)
    for m in range(P):
        if (m // 16) % 2 == 0:
            rot[m + 16, m] = -1
        else:
            rot[m - 16, m] = 1
    parts["rot"] = rot
    tok = np.arange(SEQ)
    pos = np.stack([tok // GRID_W, tok % GRID_W], -1).astype(f)
    freq = (np.float32(10000.0) ** (-np.arange(16, dtype=f) / 16)).astype(f)
    ang = pos[:, :, None] * freq
    a = ang[:, (d // 32) % 2, d % 16].T
    parts["cos"], parts["sin"] = np.cos(a).astype(f), np.sin(a).astype(f)
    r96 = np.zeros((P, MLA_QK), f)
    for m in range(NOPE, MLA_QK):
        if m < NOPE + 16:
            r96[m + 16, m] = -1
        else:
            r96[m - 16, m] = 1
    parts["rot96"] = r96
    inv = (1.0 / (np.float32(10000.0) ** (np.arange(0, ROPE, 2, dtype=f) / ROPE))).astype(f)
    a2 = (tok.astype(f)[:, None] * inv[None, :]).T
    c96, s96 = np.ones((P, SEQ), f), np.zeros((P, SEQ), f)
    for m in range(NOPE, MLA_QK):
        c96[m], s96[m] = np.cos(a2[(m - NOPE) % 16]), np.sin(a2[(m - NOPE) % 16])
    parts["cos96"], parts["sin96"] = c96, s96
    qc = (GRID_W - 1) - (i % GRID_W)
    start = np.clip(qc - NA_COLS // 2, 0, GRID_W - NA_COLS)
    kc = np.arange(GRID_W)
    win = (kc[None, :] >= start[:, None]) & (kc[None, :] < start[:, None] + NA_COLS)
    parts["win"] = win.astype(f)
    parts["notwin"] = np.where(win, 0.0, -1e9).astype(f)
    n = (SEQ - 1) - np.arange(TAB)
    nf = np.maximum(n, 1).astype(f)
    large = 16 + (np.log(nf / 16) / np.log(f(2048 / 16)) * 16).astype(np.int32)
    bucket = np.where(n < 16, np.maximum(n, 0), np.minimum(large, 31))
    hot = np.zeros((P, TAB), f)
    hot[bucket[n >= 0], np.nonzero(n >= 0)[0]] = 1.0
    hot[32, n < 0] = NEG
    parts["hot"] = hot
    at = 0
    for k, v in parts.items():
        CONST_COLS[k] = (at, at + v.shape[1])
        at += v.shape[1]
    return np.ascontiguousarray(np.concatenate(list(parts.values()), axis=1))


CONSTS = _constants()


class Tally:

    def __init__(self):
        self.n, self.term = 0, None

    def up(self, k=1):
        self.n += k
        return self.now()

    def now(self):
        return self.n if self.term is None else self.term + self.n


class Banks(Tally):

    def __init__(self, first, count):
        super().__init__()
        self.first, self.count, self.turn = first, count, None

    def take(self):
        bank = self.first + self.n % self.count
        free = self.n // self.count
        if self.turn is not None:
            free = self.turn + free
        return bank, self.up(), free


@contextmanager
def repeat(eng, turns, *tallies):
    with eng.Fori(0, turns) as i:
        before = [t.n for t, _ in tallies]
        for t, per in tallies:
            t.term = i * per
            if isinstance(t, Banks):
                assert per % t.count == 0
                t.turn = i * (per // t.count)
        yield i
        for (t, per), b in zip(tallies, before):
            assert t.n - b == per, (t.n - b, per)
            t.term = None
            if isinstance(t, Banks):
                t.turn = None
            t.n = b + per * turns


def build(nc, A, out, const, tab_dram, rows_dram, dbg=None, stop=None):
    with ExitStack() as ctx:
        def sb(name, shape):
            return ctx.enter_context(nc.sbuf_tensor(name, shape, F32))

        def sem(name):
            return ctx.enter_context(nc.semaphore(name))

        psum = [ctx.enter_context(nc.psum_tensor(f"bank{b}", [P, 512], F32)) for b in range(8)]
        hT = sb("hT", [P, DC, T])
        with nc.sbuf_tensor("scratch", [P, 2 * DC * T], F32) as scratch:
            pass
        uR = ctx.enter_context(nc.sbuf_tensor("uR", [P, 2, DC, T], F32R))
        with nc.sbuf_tensor("gR", [P, 2, F0, T], F32R) as gR:
            pass
        big = sb("big", [P, 24 * T])
        yT = sb("yT", [P, DC, T])
        wraw = sb("wraw", [P, 2, SLOT])
        wh = ctx.enter_context(nc.sbuf_tensor("wh", [P, 2, SLOT], F32R))
        wl = ctx.enter_context(nc.sbuf_tensor("wl", [P, 2, SLOT], F32R))
        cst = sb("cst", [P, CONSTS.shape[1]])
        vec = sb("vec", [P, 4, P])
        sc = sb("sc", [P, DC, 2])
        mod = sb("mod", [P, LAYERS, N_MOD * DC, 2])
        coefA = sb("coefA", [P, 6, DC, 2])
        coefG = sb("coefG", [P, 6, DC, 2])
        lams = sb("lams", [P, 8])
        warm = sb("warm", [P, 1])
        stat = sb("stat", [P, 2, 32])
        diag = sb("diag", [P, T])
        half = sb("half", [P, 2, T])
        maskb = sb("maskb", [P, 2, SEQ])
        prob = sb("prob", [P, 2, 2, T])
        probn = sb("probn", [P, 2, T])
        probT = sb("probT", [P, 2, TT, P])
        negm = sb("negm", [P, 2, 2, 2])
        rsum = sb("rsum", [P, 2, 2, 2])
        brev = sb("brev", [P, 5, SEQ])
        t5w = sb("t5w", [33, 5])
        galog = sb("galog", [P, LAYERS, 2, GH])
        gs = sb("gs", [P, 16, GN])
        vraw = prob[:, 0, :, :].rearrange("p a t -> p (a t)")[:, 0:4 * P].rearrange("p (a n) -> p a n", a=4)
        lamv = prob[:, 1, 0, 0:256]
        tline = prob[0:5, 1, 1, 0:TAB]
        sqsum = probn[:, 0, :]
        rstd = probn[:, 1, :]
        modraw = probn[0:N_MOD * DC, 0, :].rearrange("p (l s n) -> p l s n", l=LAYERS, s=2)
        sqT = scratch[:, 0:DC * T].rearrange("p (c t) -> p c t", t=T)
        hsq = scratch[:, DC * T:DC * T + 8 * SEQ].rearrange("p (c t) -> p c t", t=SEQ)
        flat = prob[:, :, :, :].rearrange("p a b t -> p (a b t)")
        wuq = flat[:, 0:2 * MLA_H * MLA_QK].rearrange("p (k n) -> p k n", k=2)
        wukv = flat[:, 2 * MLA_H * MLA_QK:2 * MLA_H * MLA_QK + 512]
        HH = NA_H // 2
        yfree = yT[:, :, :].rearrange("p a b -> p (a b)")[:, 0:3 * HH * SPAN].rearrange("p (h n) -> p h n", h=3 * HH)
        rawb = [[yfree[:, 0:HH], yfree[:, HH:2 * HH]],
                [yfree[:, 2 * HH:3 * HH], big[:, :].rearrange("p (c t) -> p c t", t=T)[:, 0:HH, 0:SPAN]]]

        def c(name):
            a, b = CONST_COLS[name]
            return cst[:, a:b]

        bigc = big[:, :].rearrange("p (c t) -> p c t", t=T)
        vtok = big[:, 16 * T:24 * T].rearrange("p (m n) -> p m n", n=D)
        adaw = big[:, :].rearrange("p (s k n) -> p s k n", s=3, k=DC)
        stage = yT[:, :, :].rearrange("p a b -> p (a b)").rearrange("p (m n) -> p m n", n=D)
        at = [0]

        def piece(store, n):
            at[0] += n
            return store[:, at[0] - n:at[0]]

        def three(ap, m):
            return ap.rearrange("p (m n) -> p m n", m=m)

        convin = three(piece(big, 12 * (SEQ + 4)), 12)
        gz = three(piece(big, 4 * SEQ), 4)
        mgate = three(piece(big, 2 * SEQ), 2)
        cgate = three(piece(big, 2 * SEQ), 2)
        attn0 = at[0]
        mbq = three(piece(big, 2 * SEQ), 2)
        mbk = three(piece(big, 2 * SEQ), 2)
        mbv = three(piece(big, 2 * SEQ), 2)
        cq = three(piece(big, 2 * SEQ), 2)
        ckv = piece(big, SEQ)
        mq = three(piece(big, MLA_H * SEQ), MLA_H)
        mk = three(piece(big, MLA_H * SEQ), MLA_H)
        mv = three(piece(big, 2 * 256), 2)
        attn1 = at[0]
        yc = three(piece(big, DC * SEQ), DC)
        assert at[0] <= 24 * T
        at[0] = 0
        ktok = three(piece(big, GN * P), GN)
        vtk = three(piece(big, GN * P), GN)
        at[0] = attn0
        Xm = three(piece(big, GN * P), GN)
        XT = three(piece(big, GN * P), GN)
        Ym = three(piece(big, GN * P), GN)
        LT = three(piece(big, GN * P), GN)
        assert at[0] <= attn1
        DTm, ATm = hT[:, :, 0:P], hT[:, :, P:2 * P]
        at[0] = 0
        yflat = yT[:, :, :].rearrange("p a b -> p (a b)")
        cvo = three(piece(yflat, 12 * SEQ), 12)
        EG = three(piece(yflat, GH * P), GH)
        qg = EG
        S1 = three(piece(yflat, GH * P), GH)
        rflat = scratch[:, :]
        at[0] = 0
        LmT = three(piece(rflat, GN * P), GN)
        gB = three(piece(rflat, GN * P), GN)
        Rm = three(piece(rflat, GN * P), GN)
        Um = three(piece(rflat, GN * P), GN)
        prt = prob[:, :, :, :].rearrange("p a b t -> p (a b t)")
        oraw = three(prt[:, 0:GH * SEQ], GH)

        def v_norm(l, g):
            return vec[:, 0, (l * 6 + g) * DC:(l * 6 + g + 1) * DC]

        V_C, V_CC, V_NW = 96, 104, 112
        V_FIN, V_SUB, V_Q, V_KV, V_GN = 72, 80, 81, 85, 87

        x_in = sem("x_in")
        const_in = sem("const_in")
        vec_in = sem("vec_in")
        misc_in = sem("misc_in")
        rawb_in = sem("rawb_in")
        ada_in = [sem(f"ada_in{s}") for s in range(3)]
        w_in = [sem(f"w_in{s}") for s in range(2)]
        w_hi = sem("w_hi")
        w_lo = sem("w_lo")
        ada_free = sem("ada_free")
        ada_done = sem("ada_done")
        rows_out = [sem(f"rows_out{b}") for b in range(2)]
        mod_in = sem("mod_in")
        mla_in = sem("mla_in")
        y_added = sem("y_added")
        gm_ready = sem("gm_ready")
        gh_ready = sem("gh_ready")
        head_ready = sem("head_ready")
        uh_ready = sem("uh_ready")
        line_out = sem("line_out")
        brev_in = sem("brev_in")
        out_done = sem("out_done")
        gemm_full = sem("gemm_full")
        gemm_free = [sem(f"gemm_free{b}") for b in range(4)]
        small_full = sem("small_full")
        small_free = [sem(f"small_free{b}") for b in range(2)]
        pv_done = sem("pv_done")
        o_taken = sem("o_taken")
        vec_step = sem("vec_step")
        act_step = sem("act_step")
        t5_set = sem("t5_set")
        h_ready = sem("h_ready")
        vec_ready = sem("vec_ready")
        sc_ready = sem("sc_ready")
        line_ready = sem("line_ready")
        sq_ready = sem("sq_ready")
        var_ready = sem("var_ready")
        root_ready = sem("root_ready")
        diag_ready = sem("diag_ready")
        n_ready = sem("n_ready")
        u_ready = sem("u_ready")
        silu_ready = sem("silu_ready")
        g_ready = sem("g_ready")
        qkv_ready = sem("qkv_ready")
        rope_ready = sem("rope_ready")
        bias_ready = sem("bias_ready")
        negm_ready = sem("negm_ready")
        exp_ready = sem("exp_ready")
        probn_ready = sem("probn_ready")
        probT_ready = sem("probT_ready")
        o_ready = sem("o_ready")
        lam_in = sem("lam_in")
        lam_exp = sem("lam_exp")
        out_ready = sem("out_ready")
        a_act = sem("a_act")
        v_hyb = sem("v_hyb")

        sum_ready = sem("sum_ready")
        v_ready = sem("v_ready")
        on_ready = sem("on_ready")
        block = ctx.enter_context(nc.Block())

        def da_items():
            for h in range(8):
                for t in range(TT):
                    nk = CTX if t < CTX // P else T
                    yield dict(
                        q=[bigc[64 * j:64 * j + 64, h, t * P:t * P + P] for j in range(2)],
                        k=[bigc[64 * j:64 * j + 64, 8 + h, 0:nk] for j in range(2)], nk=nk, scale=0.125,
                        v=[vtok[:, kt, h * P:h * P + P] for kt in range(nk // P)], rows=(0, P), cols=t * P)

        def na_items():
            for h in range(NA_H):
                r = 64 * (h % 2)
                for t in range(SEQ // P):
                    yield dict(
                        q=[bigc[r:r + 64, h // 2, CTX + t * P:CTX + t * P + P]], k=[bigc[r:r + 64, 8 + h // 2, :]],
                        nk=T, scale=1.0, na=(h, t),
                        v=[vtok[:, kt, h * 64:h * 64 + 64] for kt in range(TT)], rows=(r, r + 64), cols=t * P)

        def mla_items():
            for h in range(MLA_H):
                r = 64 * (h % 2)
                for t in range(2):
                    nk = (t + 1) * P
                    yield dict(q=[mq[0:MLA_QK, h, t * P:t * P + P]], k=[mk[0:MLA_QK, h, 0:nk]], nk=nk, scale=1.0,
                               bias=brev[:, 4, P * (1 - t):P * (1 - t) + nk],
                               v=[mv[:, kt, h * 64:h * 64 + 64] for kt in range(t + 1)], rows=(r, r + 64), cols=t * P)

        def moba_items():
            for h in range(4):
                r = 64 * (h % 2)
                for t in range(2):
                    nk = (t + 1) * P
                    yield dict(q=[mbq[r:r + 64, h // 2, t * P:t * P + P]], k=[mbk[r:r + 64, h // 2, 0:nk]], nk=nk,
                               scale=1.0, bias=brev[:, h, P * (1 - t):P * (1 - t) + nk],
                               v=[mbv[:, kt, h * 64:h * 64 + 64] for kt in range(t + 1)], rows=(r, r + 64),
                               cols=t * P)

        def item_base(counter, n):
            counter[0] += n
            return counter[0] - n

        HY = [(0, 256), (256, 160), (416, 256)] + [(672 + 256 * b, 256) for b in range(8)] + \
             [(2720, 8), (2728, 256), (2984, 256), (3240, 256), (3496, 256)]

        STAGES = ["ada", "ffn00", "da", "ffn01", "ffn10", "na", "ffn11", "hy0", "hy1"]
        run = STAGES if stop is None else STAGES[:STAGES.index(stop) + 1]

        SIZES = []
        for st in run:
            if st.startswith("ffn"):
                for kc in (F0, FC - F0):
                    SIZES += kc * [DC * 2 * P] + DC * [kc * P]
            elif st in ("da", "na"):
                SIZES += 16 * [DC * 256]
            elif st.startswith("hy"):
                SIZES += [DC * w for _, w in HY] + 4 * [DC * 256]
        if stop is not None and not stop.startswith("hy"):
            SIZES += 2 * [SLOT]
        U_BEFORE_NA = 5 * 2 * DC
        U_BEFORE_HY1 = U_BEFORE_NA + 2 * DC + 4

        @block.sync
        def _(sp):
            sp.dma_start(cst[:, :], const).then_inc(const_in, 16)
            sp.dma_start(stage[:, 0:2, :], A["ctx"][0].rearrange("(m p) n -> p m n", p=P)).then_inc(x_in, 16)
            sp.dma_start(stage[:, 2:4, :], A["x"][0].rearrange("(m p) n -> p m n", p=P)).then_inc(x_in, 16)
            rows = [(0, 0, A["norm_g"].rearrange("l g (c p) -> (l g c) p", p=P)),
                    (0, V_C, A["c"].rearrange("o (c p) -> (o c) p", p=P)),
                    (0, V_CC, A["c_ctx"].rearrange("(c p) -> c p", p=P)),
                    (0, V_NW, A["norm_w_2"].rearrange("l (c p) -> (l c) p", p=P)),
                    (1, 0, A["ada_b"][0].rearrange("(c p) -> c p", p=P)),
                    (2, 0, A["ada_b"][1].rearrange("(c p) -> c p", p=P)),
                    (1, V_FIN, A["final_norm_w_2"].rearrange("(c p) -> c p", p=P)),
                    (1, V_SUB, A["da_subln_g"]),
                    (1, V_Q, A["mla_q_norm_2"].rearrange("l (c p) -> (l c) p", p=P)),
                    (1, V_KV, A["mla_kv_norm_2"]),
                    (1, V_GN, A["gdn_norm_w_2"]),
                    (3, 0, A["gdn_conv_w_2"].rearrange("l j (c p) -> (l j c) p", p=P))]
            for tile, r, src in rows:
                sp.dma_start(vraw[r:r + src.shape[0], tile, :], src).then_inc(vec_in, 16)
            views = [A["ada_w"][l].rearrange("(k p) n -> p k n", p=P) for l in range(LAYERS)]
            for l in range(LAYERS):
                if l == 0:
                    for s in range(3):
                        sp.dma_start(adaw[:, s], views[0][:, :, s * 512:(s + 1) * 512]).then_inc(ada_in[s], 16)
                    sp.dma_start(lamv, A["da_lambda"][0].rearrange("(o a) b -> o (a b)", o=1).to_broadcast([P, 256])).then_inc(lam_in, 16)
                    sp.dma_start(t5w[0:32, 0:4], A["t5_table_2"]).then_inc(misc_in, 16)
                    for k in range(LAYERS):
                        sp.dma_start(galog[:, k, 0], A["gdn_A_log_2"][k:k + 1, :].to_broadcast([P, GH])).then_inc(misc_in, 16)
                        sp.dma_start(galog[:, k, 1], A["gdn_dt_bias_2"][k:k + 1, :].to_broadcast([P, GH])).then_inc(misc_in, 16)
                first = 1 if l == 0 else 0
                with sp.Fori(first, 6) as i:
                    for s in range(3):
                        sp.wait_ge(ada_done, (i * 3 + (18 * l - 2 + s)))
                        sp.dma_start(adaw[:, s], views[l][:, :, bass.ds(i * 1536 + s * 512, 512)]).then_inc(ada_in[s], 16)

            def small_tables():
                for b in range(2):
                    sp.wait_ge(rows_out[b], 16 + 16 * 9 * LAYERS)
                for l in range(LAYERS):
                    sp.dma_start(modraw[:, l], rows_dram[l].rearrange("s (c n) -> c s n", n=P)).then_inc(mod_in, 16)
                sp.wait_ge(line_ready, 1)
                sp.dma_start(tab_dram, tline).then_inc(line_out, 16)
                sp.wait_ge(line_out, 16)
                src = bass.AP(tensor=tab_dram.tensor, offset=tab_dram.offset, ap=[[1, P], [TAB, 5], [1, SEQ]])
                sp.dma_start(brev[:, :, :], src).then_inc(brev_in, 16)

            nblk = Tally()

            def block_in(s, pairs):
                b = nblk.now()
                if not isinstance(b, int) or b >= 2:
                    sp.wait_ge(w_lo, b - 1)
                nblk.up()
                for dst, src in pairs:
                    sp.dma_start(dst, src).then_inc(w_in[s], 16)

            def stream(n, parts):
                assert n % 2 == 0 and nblk.n % 2 == 0
                if n <= 4:
                    for b in range(n):
                        block_in(b % 2, parts(b % 2, b))
                    return
                if nblk.n == 0:
                    for b in range(2):
                        block_in(b, parts(b, b))
                    small_tables()
                    first = 1
                else:
                    first = 0
                with sp.Fori(first, n // 2) as i:
                    base = nblk.n
                    nblk.term = (i - first) * 2
                    for s in range(2):
                        block_in(s, parts(s, i * 2 + s))
                    nblk.term = None
                    nblk.n = base + n - 2 * first

            def cut(view, b, width, c0=0):
                if isinstance(b, int):
                    return view[:, :, c0 + b * width:c0 + (b + 1) * width]
                return view[:, :, bass.ds(b * width + c0, width)]

            def slot_of(s, kc, width):
                return wraw[:, s, 0:kc * width].rearrange("p (k n) -> p k n", k=kc)

            def columns(view, kc, width, c0=0):
                m = kc // 2
                return lambda s, b: [(slot_of(s, kc, width)[:, 0:m], cut(view, b, width, c0)[:, 0:m]),
                                     (slot_of(s, kc, width)[:, m:kc], cut(view, b, width, c0)[:, m:kc])]

            for st in run:
                if st.startswith("ffn"):
                    l, half_ = int(st[3]), int(st[4])
                    w1 = A["ffn_w_in"][l, half_].rearrange("(k p) n -> p k n", p=P)
                    w2 = A["ffn_w_out"][l, half_].rearrange("(k p) n -> p k n", p=P)
                    for k0, kc in ((0, F0), (F0, FC - F0)):
                        def gates(s, b, k0=k0):
                            slot = wraw[:, s, :].rearrange("p (k a n) -> p k a n", k=DC, a=2)
                            return [(slot[:, :, a], cut(w1, b, P, k0 * P + a * F)) for a in range(2)]
                        stream(kc, gates)
                        stream(DC, columns(w2[:, k0:k0 + kc], kc, P))
                elif st in ("da", "na"):
                    w = A[st + "_w_in"][0].rearrange("(k p) n -> p k n", p=P)
                    stream(4, columns(w, DC, 256))
                    if st == "na":
                        sp.wait_ge(u_ready, U_BEFORE_NA)
                        base = A["na_rpb"][0, 0, 0, 0:1]
                        for t in range(2):
                            for rr in range(2):
                                r = 2 * t + 1 - rr
                                for hh in range(2):
                                    at_ = base.offset + (hh * HH * RPB_R + NA_ROWS - 1 - r) * RPB_C + NA_COLS - GRID_W
                                    src = bass.AP(tensor=base.tensor, offset=at_,
                                                  ap=[[1, GRID_W], [RPB_R * RPB_C, HH], [1, SPAN]])
                                    sp.dma_start(rawb[t][hh][64 * rr:64 * rr + 64], src).then_inc(rawb_in, 16)
                    stream(8, columns(w, DC, 256, 4 * 256))
                    stream(4, columns(A[st + "_w_out"][0].rearrange("(k p) n -> p k n", p=P), DC, 256))
                elif st.startswith("hy"):
                    l = int(st[2])
                    w = A["w_in_2"][l].rearrange("(k p) n -> p k n", p=P)
                    for n, (c0, width) in enumerate(HY):
                        block_in(n % 2, columns(w, DC, width, c0)(n % 2, 0))
                        if n == 1:
                            if l == 0:
                                sp.wait_ge(on_ready, 16)
                            else:
                                sp.wait_ge(u_ready, U_BEFORE_HY1)
                            sp.dma_start(wuq, A["mla_w_uq_2"][l].rearrange("(a p) n -> p a n", p=P)).then_inc(mla_in, 16)
                            sp.dma_start(wukv, A["mla_w_ukv_2"][l]).then_inc(mla_in, 16)
                    w = A["w_out_2"][l].rearrange("(k p) n -> p k n", p=P)
                    for b in range(4):
                        block_in(b % 2, columns(w, DC, 256)(b % 2, b))
            if len(SIZES) > nblk.n:
                stream(2, columns(views[0], DC, 256))
            sp.wait_ge(out_ready, 1)
            if dbg is not None:
                sp.wait_ge(out_ready, 2)
                sp.dma_start(dbg, hT[:, :, :]).then_inc(out_done, 16)
                sp.wait_ge(out_done, 16)
            if stop is None:
                sp.dma_start(out[0].rearrange("(m p) n -> p m n", p=P), stage[:, 0:2, :]).then_inc(out_done, 16)
                sp.wait_ge(out_done, 16)

        def rep(ap, m):
            return bass.AP(tensor=ap.tensor, offset=ap.offset, ap=[ap.ap[0], [0, m], ap.ap[1]])

        def wide(ap, m):
            return bass.AP(tensor=ap.tensor, offset=ap.offset, ap=[ap.ap[0], ap.ap[1], [0, m]])

        def shape_of(st):
            return (CTX, [1]) if st in ("ffn11", "na") else (0, [0, 1])

        SUB = {"ffn00": (0, 0), "da": (0, 1), "ffn01": (0, 2), "ffn10": (1, 0), "na": (1, 1), "ffn11": (1, 2)}
        ident, flip, ones, upto = c("ident"), c("flip"), c("ones"), c("upto")
        STEPS = MLA_QK ** -0.5
        SPREAD_AT = [2, 5, 8, 11]

        @block.tensor
        def _(pe):
            gemm, small, opsum = Banks(0, 4), Banks(4, 2), Banks(6, 2)
            tl = {k: Tally() for k in ("u", "g", "w", "sq", "sum", "diag", "qkv", "v", "probn", "probT", "bias", "on",
                                       "vh", "aa")}
            mm = nc.tensor.matmul

            def bank(pool, frees):
                b, full, free = pool.take()
                if not (isinstance(free, int) and free == 0):
                    pe.wait_ge(frees[b - pool.first], free)
                return psum[b]

            def gbank():
                return bank(gemm, gemm_free)

            def sbank():
                return bank(small, small_free)

            def stats(groups, nt):
                o = sbank()
                for g, parts in enumerate(groups):
                    for t in range(nt):
                        for k, a in enumerate(parts):
                            ins = mm(o[:, g * nt + t:g * nt + t + 1], a[:, t * P:t * P + P], ones[:, 0:1],
                                     start=(k == 0), stop=(k == len(parts) - 1))
                ins.then_inc(small_full, 1)

            def spread(n):
                pe.wait_ge(diag_ready, tl["diag"].up())
                o = sbank()
                mm(o[:, 0:n], ones, diag[:, 0:n], start=True, stop=True).then_inc(small_full, 1)

            def prenorm(c0):
                o = sbank()
                for k in range(DC):
                    pe.wait_ge(sq_ready, tl["sq"].up())
                    ins = mm(o[:, 0:T - c0], ones, yT[:, k, c0:T], start=(k == 0), stop=(k == DC - 1))
                ins.then_inc(small_full, 1)

            def postnorm(c0):
                pe.wait_ge(sum_ready, tl["sum"].up())
                stats([[sqsum[:, c0:T]]], (T - c0) // P)
                spread(T - c0)
                tl["sq"].up(DC)

            def product3(o, parts):
                for n, (a, b, wait) in enumerate(parts):
                    if wait is not None:
                        pe.wait_ge(*wait)
                    mm(o, a[0], b[0], start=(n == 0), stop=False)
                    mm(o, a[0], b[1], start=False, stop=False)
                    ins = mm(o, a[1], b[0], start=False, stop=(n == len(parts) - 1))
                return ins

            def weights(s, kc, width):
                pe.wait_ge(w_lo, tl["w"].up())
                return [w[:, s, 0:kc * width].rearrange("p (k n) -> p k n", k=kc) for w in (wh, wl)]

            def both(pair, *at):
                return [x[(slice(None), *at)] for x in pair]

            u2 = (uR[:, 0], uR[:, 1])
            g2 = (gR[:, 0], gR[:, 1])

            def out_proj(src, c0, kc, width, blocks, ready, r0):
                with repeat(pe, blocks // 4, (gemm, 4 * width // P), (tl["w"], 4)) as i:
                    for b in range(4):
                        w = weights(b % 2, kc, width)
                        for j in range(width // P):
                            o = gbank()
                            first = b == 0 and j == 0
                            product3(o[:, 0:T - c0],
                                     [(both(w, k, slice(j * P, j * P + P)), both(src, k, slice(c0, T)),
                                       (ready, r0 + k + 1) if first else None)
                                      for k in range(kc)]).then_inc(gemm_full, 1)

            def attention(items, spread_at=()):
                items = list(items)

                def scores(it):
                    for q, k in zip(it["q"], it["k"]):
                        o = gbank()
                        nk = it["nk"]
                        if "bias" in it:
                            mm(o[:, 0:nk], q, k, start=True, stop=False)
                            ins = mm(o[:, 0:nk], flip, it["bias"], start=False, stop=True)
                        elif "na" in it:
                            mm(o[:, 0:nk], q, k, start=True, stop=False)
                            pe.wait_ge(bias_ready, tl["bias"].up())
                            ins = mm(o[:, CTX:T], flip, maskb[:, it["na"][1], :], start=False, stop=True)
                        else:
                            ins = mm(o[:, 0:nk], q, k, start=True, stop=True)
                        ins.then_inc(gemm_full, 1)

                def turn(i, it):
                    pe.wait_ge(probn_ready, tl["probn"].up())
                    o = sbank()
                    for kt in range(it["nk"] // P):
                        ins = nc.tensor.transpose(o[:, kt * P:kt * P + P], probn[:, i % 2, kt * P:kt * P + P], ident)
                    ins.then_inc(small_full, 1)

                def values(i, it):
                    if i % 4 == 0:
                        b, full, free = opsum.take()
                        obank[0] = psum[b]
                        if opsum.n > 2:
                            pe.wait_ge(o_taken, opsum.n - 2)
                    pe.wait_ge(probT_ready, tl["probT"].up())
                    r0, r1 = it["rows"]
                    for kt, v in enumerate(it["v"]):
                        ins = mm(obank[0][r0:r1, it["cols"]:it["cols"] + P], v, probT[:, i % 2, kt, :],
                                 start=(kt == 0), stop=(kt == len(it["v"]) - 1))
                    ins.then_inc(pv_done, 1)

                obank = [None]
                scores(items[0])
                scores(items[1])
                for i, it in enumerate(items):
                    if i + 2 < len(items):
                        scores(items[i + 2])
                    turn(i, it)
                    if i in spread_at:
                        spread(T)
                    if i:
                        values(i - 1, items[i - 1])
                values(len(items) - 1, items[-1])

            def hybrid(l):
                def step_v(k=1):
                    pe.wait_ge(v_hyb, tl["vh"].up(k))

                def step_a(k=1):
                    pe.wait_ge(a_act, tl["aa"].up(k))

                prenorm(CTX)
                tl["vh"].up()
                u0 = tl["u"].n
                tl["u"].up(DC)
                for n, (c0, width) in enumerate(HY):
                    w = weights(n % 2, DC, width)
                    o = gbank()
                    if n in (11, 14):
                        for t in range(2):
                            ins = product3(o[:, t * width:t * width + width],
                                           [(both(u2, k, slice(CTX + t * P, CTX + t * P + P)), both(w, k), None)
                                            for k in range(DC)])
                    else:
                        cols = {1: [(0, P), (64, 160)]}.get(n, [(0, P), (P, 2 * P)])
                        for j, (a, b) in enumerate(cols):
                            ins = product3(o[0:b - a, j * SEQ:j * SEQ + SEQ],
                                           [(both(w, k, slice(a, b)), both(u2, k, slice(CTX, T)),
                                             (u_ready, u0 + k + 1) if n == 0 and j == 0 else None)
                                            for k in range(DC)])
                    ins.then_inc(gemm_full, 1)
                step_a()
                o = sbank()
                for t in range(2):
                    for k in range(2):
                        mm(o[:, t:t + 1], half[:, 0, k * SEQ + t * P:k * SEQ + t * P + P], ones[:, 0:1],
                           start=(k == 0), stop=(k == 1))
                for t in range(2):
                    ins = mm(o[:, 2 + t:3 + t], half[:, 1, t * P:t * P + P], ones[:, 0:1], start=True, stop=True)
                ins.then_inc(small_full, 1)
                spread(SEQ)
                spread(SEQ)
                step_v(3)
                pe.wait_ge(mla_in, 32 * (l + 1))
                for p in range(2):
                    o = gbank()
                    for j in range(2):
                        h = 2 * p + j
                        for k in range(2):
                            ins = mm(o[0:MLA_QK, j * SEQ:j * SEQ + SEQ], wuq[:, k, h * MLA_QK:(h + 1) * MLA_QK],
                                     cq[:, k, :], start=(k == 0), stop=(k == 1))
                    ins.then_inc(gemm_full, 1)
                for p in range(2):
                    o = gbank()
                    for j in range(2):
                        h = 2 * p + j
                        ins = mm(o[0:NOPE, j * SEQ:j * SEQ + SEQ], wukv[:, h * P:h * P + NOPE], ckv,
                                 start=True, stop=True)
                    ins.then_inc(gemm_full, 1)
                for t in range(2):
                    o = gbank()
                    mm(o[:, :], ckv[:, t * P:t * P + P], wukv[:, :], start=True, stop=True).then_inc(gemm_full, 1)
                step_a()
                for p in range(2):
                    step_a()
                    o = sbank()
                    mm(o[0:MLA_QK, :], c("rot96")[0:MLA_QK, :], mq[0:MLA_QK, 2 * p:2 * p + 2, :],
                       start=True, stop=True).then_inc(small_full, 1)
                step_a(2)
                o = sbank()
                mm(o[0:MLA_QK, 0:SEQ], c("rot96")[0:MLA_QK, :], mk[0:MLA_QK, 0, :], start=True,
                   stop=True).then_inc(small_full, 1)
                stats([[hsq[:, g, :]] for g in range(8)], 2)
                step_v(5)
                if l == 0:
                    pe.wait_ge(brev_in, 16)
                attention([*mla_items(), *moba_items()], SPREAD_AT)
                step_v(1 + 4)
                for src in (4, 8):
                    for t in range(2):
                        o = gbank()
                        for h in range(GH):
                            ins = nc.tensor.transpose(o[:, h * P:h * P + P], cvo[:, src + h, t * P:t * P + P], ident)
                        ins.then_inc(gemm_full, 1)
                o = sbank()
                mm(o[:, 0:GN], upto, gs[:, 9, :], start=True, stop=True).then_inc(small_full, 1)
                for t in range(2):
                    o = gbank()
                    for h in range(GH):
                        ins = mm(o[:, h * P:h * P + P], gB[:, 4 * t + h, :], upto, start=True, stop=True)
                    ins.then_inc(gemm_full, 1)
                for first in (4, 0):
                    for t in range(2):
                        o = gbank()
                        for h in range(GH):
                            ins = mm(o[:, h * P:h * P + P], cvo[:, 4 + h, t * P:t * P + P],
                                     cvo[:, first + h, t * P:t * P + P], start=True, stop=True)
                        ins.then_inc(gemm_full, 1)
                step_v(2)
                for t in range(2):
                    o = gbank()
                    for h in range(GH):
                        ins = nc.tensor.transpose(o[:, h * P:h * P + P], LT[:, 4 * t + h, :], ident)
                    ins.then_inc(gemm_full, 1)
                step_v()
                for t in range(2):
                    o = gbank()
                    for h in range(GH):
                        ins = nc.tensor.transpose(o[:, h * P:h * P + P], Ym[:, 4 * t + h, :], ident)
                    ins.then_inc(gemm_full, 1)
                step_a(4)
                for m in range(1, LEVELS):
                    for t in range(2):
                        if m > 1 or t == 0:
                            step_v(2 - t if m > 1 else 1)
                        o = gbank()
                        for h in range(GH):
                            n = 4 * t + h
                            ins = mm(o[:, h * P:h * P + P], LmT[:, n, :], Xm[:, n, :], start=True, stop=True)
                        ins.then_inc(gemm_full, 1)
                    for t in range(2):
                        step_a()
                        for which in range(2):
                            if which == 0 and m == LEVELS - 1:
                                continue
                            o = gbank()
                            for h in range(GH):
                                n = 4 * t + h
                                ins = mm(o[:, h * P:h * P + P], *((XT[:, n, :], Ym[:, n, :]) if which == 0 else
                                                                 (Ym[:, n, :], XT[:, n, :])), start=True, stop=True)
                            ins.then_inc(gemm_full, 1)
                step_v(2)

                def tiles(f):
                    o = gbank()
                    for h in range(GH):
                        pairs = f(h)
                        for k, (a, b) in enumerate(pairs):
                            ins = mm(o[:, h * P:h * P + P], a, b, start=(k == 0), stop=(k == len(pairs) - 1))
                    ins.then_inc(gemm_full, 1)

                tiles(lambda h: [(XT[:, h, :], vtk[:, h, :])])
                step_a()
                tiles(lambda h: [(ktok[:, h, :], Um[:, h, :])])
                tiles(lambda h: [(Um[:, h, :], ATm[:, h, :])])
                step_a()
                tiles(lambda h: [(cvo[:, 4 + h, P:2 * P], S1[:, h, :])])
                step_v()
                tiles(lambda h: [(XT[:, 4 + h, :], Rm[:, 4 + h, :])])
                step_a(2)
                tiles(lambda h: [(S1[:, h, :], qg[:, h, :]), (Um[:, 4 + h, :], ATm[:, 4 + h, :])])
                step_a()
                stats([[hsq[:, g, :]] for g in range(4)], 2)
                for p in range(2):
                    spread(T)
                tl["vh"].up(2)
                u0 = tl["u"].n
                tl["u"].up(4)
                for b in range(4):
                    w = weights(b % 2, DC, 256)
                    o = gbank()
                    for j in range(2):
                        ins = product3(o[:, j * SEQ:j * SEQ + SEQ],
                                       [(both(w, k, slice(j * P, j * P + P)), both(u2, k, slice(CTX, T)),
                                         (u_ready, u0 + n // 2 + 1) if b == 0 and j == 0 else None)
                                        for n, k in enumerate((0, 1, 6, 7, 2, 3, 4, 5))])
                    ins.then_inc(gemm_full, 1)

            tl["g"].up(2)
            pe.wait_ge(const_in, 16)
            pe.wait_ge(vec_in, 16 * 12)
            o = sbank()
            for j, r in enumerate((128, 89, 72, 96)):
                ins = nc.tensor.transpose(o[:, j * P:j * P + r], vraw[0:r, j, :], ident[0:r, 0:r])
            ins.then_inc(small_full, 1)
            pe.wait_ge(x_in, 32)
            for k in range(DC):
                o = gbank()
                for t in range(TT):
                    ins = nc.tensor.transpose(o[:, t * P:t * P + P], stage[:, t, k * P:k * P + P], ident)
                ins.then_inc(gemm_full, 1)
            pe.wait_ge(misc_in, 16 * 5)
            pe.wait_ge(t5_set, 1)
            o = sbank()
            mm(o[0:5, 0:TAB], t5w[:, :], c("hot")[0:33, :], start=True, stop=True).then_inc(small_full, 1)
            pe.wait_ge(sc_ready, 1)
            abank = Banks(6, 2)
            for l in range(LAYERS):
                with repeat(pe, 3, (abank, 6)) as i:
                    for b in range(6):
                        s = b % 3
                        pe.wait_ge(ada_in[s], i * 32 + (6 * l + b // 3 + 1) * 16)
                        bank_no, full, _ = abank.take()
                        pe.wait_ge(ada_free, full)
                        for k in range(DC):
                            ins = mm(psum[bank_no][0:2, :], sc[:, k, :], adaw[:, s, k, :],
                                     start=(k == 0), stop=(k == DC - 1))
                        ins.then_inc(ada_done, 1)
            pe.wait_ge(mod_in, 32)
            o = sbank()
            for l in range(LAYERS):
                for s in range(2):
                    a = (2 * l + s) * N_MOD * DC
                    ins = nc.tensor.transpose(o[:, a:a + N_MOD * DC], modraw[:, l, s, :],
                                              ident[0:N_MOD * DC, 0:N_MOD * DC])
            ins.then_inc(small_full, 1)

            for st in run:
                c0, streams = shape_of(st)
                if st.startswith("ffn"):
                    prenorm(c0)
                    u0 = tl["u"].n
                    tl["u"].up(DC * len(streams))
                    for part, kc in enumerate((F0, FC - F0)):
                        with repeat(pe, kc // 2, (gemm, 4), (tl["w"], 2)) as i:
                            for s in range(2):
                                w = weights(s, DC, 2 * P)
                                for a in range(2):
                                    o = gbank()
                                    first = part == 0 and s == 0 and a == 0
                                    product3(o[:, 0:T - c0],
                                             [(both(w, k, slice(a * P, a * P + P)), both(u2, k, slice(c0, T)),
                                               (u_ready, u0 + len(streams) * (k + 1)) if first else None)
                                              for k in range(DC)]).then_inc(gemm_full, 1)
                        g0 = tl["g"].n
                        tl["g"].up(kc)
                        out_proj(g2, c0, kc, P, DC, g_ready, g0)
                    postnorm(c0)
                elif st in ("da", "na"):
                    prenorm(0)
                    u0 = tl["u"].n
                    tl["u"].up(DC * 2)
                    for q0 in (c0, 0):
                        with repeat(pe, 2, (gemm, 4), (tl["w"], 2)) as i:
                            for s in range(2):
                                w = weights(s, DC, 256)
                                for j in range(2):
                                    o = gbank()
                                    first = s == 0 and j == 0
                                    product3(o[:, 0:T - q0],
                                             [(both(w, k, slice(j * P, j * P + P)), both(u2, k, slice(q0, T)),
                                               (u_ready, u0 + 2 * (k + 1)) if first else None)
                                              for k in range(DC)]).then_inc(gemm_full, 1)
                    pe.wait_ge(qkv_ready, tl["qkv"].up(16))
                    more = [(small, 8)] if st == "da" else []
                    with repeat(pe, 2, (gemm, 8), (tl["w"], 2), *more) as i:
                        for s in range(2):
                            w = weights(s, DC, 256)
                            for t in range(TT):
                                o = gbank()
                                product3(o[:, 0:256], [(both(u2, k, slice(t * P, t * P + P)), both(w, k), None)
                                                       for k in range(DC)]).then_inc(gemm_full, 1)
                                if st == "da":
                                    o = sbank()
                                    mm(o[:, 0:SEQ], c("rot"), bigc[:, bass.ds(i * 8 + s * 4 + t, 1), CTX:T],
                                       start=True, stop=True).then_inc(small_full, 1)
                    pe.wait_ge(v_ready, tl["v"].up(16))
                    if st == "da":
                        pe.wait_ge(rope_ready, 16)
                    attention(da_items() if st == "da" else na_items())
                    if st == "da":
                        pe.wait_ge(sq_ready, tl["sq"].up(8))
                        stats([[sqT[:, h, :]] for h in range(8)], TT)
                        for h in range(8):
                            spread(T)
                    on0 = tl["on"].n
                    tl["on"].up(8)
                    out_proj(u2, c0, DC, 256, 4, on_ready, on0)
                    postnorm(c0)
                elif st.startswith("hy"):
                    hybrid(int(st[2]))
            if stop is None:
                prenorm(CTX)
                pe.wait_ge(v_hyb, tl["vh"].up())
                for t in range(2):
                    for g in range(2):
                        o = gbank()
                        for j in range(4):
                            ins = nc.tensor.transpose(o[:, j * P:j * P + P],
                                                      bigc[:, 4 * g + j, CTX + t * P:CTX + t * P + P], ident)
                        ins.then_inc(gemm_full, 1)

        @block.scalar
        def _(act):
            gemm, small = Banks(0, 4), Banks(4, 2)
            own = Tally()
            tl = {k: Tally() for k in ("h", "var", "n", "g", "gm", "sq", "negm", "probn", "pv", "o", "vh", "aa", "head",
                                       "yadd", "w0", "w1", "split")}

            def do(ins, *signals):
                ins.then_inc(act_step, 1)
                act.wait_ge(act_step, own.up())
                for s in signals:
                    act.sem_inc(s, 1)

            A_ = nc.scalar.activation

            def product(pool=None):
                pool = pool or gemm
                b, full, _ = pool.take()
                act.wait_ge(gemm_full if pool is gemm else small_full, full)
                return psum[b], (gemm_free if pool is gemm else small_free)[b - pool.first]

            def warm_root():
                do(A_(warm[:, :], c("ones")[:, 0:1], ACT.Sqrt))

            def root(n):
                act.wait_ge(var_ready, tl["var"].up())
                do(A_(stat[:, 0, 0:n], stat[:, 0, 0:n], ACT.Sqrt), root_ready)

            def root_wide(streams):
                for s in streams:
                    act.wait_ge(var_ready, tl["var"].up())
                    r = rstd[:, s * CTX:s * CTX + SEQ]
                    do(A_(r, r, ACT.Sqrt), root_ready)

            def squares(c0):
                for k in range(DC):
                    act.wait_ge(h_ready, tl["h"].up())
                    A_(yT[:, k, c0:T], hT[:, k, c0:T], ACT.Square).then_inc(sq_ready, 1)

            def shift(l, sub, streams):
                for k in range(DC):
                    for s in streams:
                        act.wait_ge(n_ready, tl["n"].up())
                        a = slice(s * CTX, s * CTX + SEQ)
                        A_(uR[:, 0, k, a], yT[:, k, a], ACT.Identity,
                           bias=mod[:, l, 3 * sub * DC + k, s:s + 1]).then_inc(uh_ready, 1)

            def lead(s, n=SLOT):
                act.wait_ge(gemm_full, gemm.now())
                act.wait_ge(w_in[s], tl["w0" if s == 0 else "w1"].up(32))
                tl["split"].up()
                do(A_(wh[:, s, 0:n], wraw[:, s, 0:n], ACT.Copy), w_hi)

            def lead_next():
                b = tl["split"].n
                if b < len(SIZES):
                    lead(b % 2, SIZES[b])

            def split_heads(c0):
                for k in range(DC):
                    act.wait_ge(head_ready, tl["head"].up())
                    A_(uR[:, 0, k, c0:T], bigc[:, k, c0:T], ACT.Copy).then_inc(uh_ready, 1)

            def attention(items, spread_at=()):
                items = list(items)

                def exps(i, it):
                    act.wait_ge(negm_ready, tl["negm"].up())
                    if i >= 2:
                        act.wait_ge(probn_ready, tl["probn"].now() + i - 1)
                    for j in range(len(it["q"])):
                        o, free = product()
                        do(A_(prob[:, i % 2, j, 0:it["nk"]], o[:, 0:it["nk"]], ACT.Exp, bias=negm[:, i % 2, 1, j:j + 1],
                              scale=it["scale"], accum_out=rsum[:, i % 2, 0, j:j + 1]), free)
                    act.sem_inc(exp_ready, 1)

                def turned(i, it):
                    o, free = product(small)
                    if i >= 2:
                        act.wait_ge(pv_done, tl["pv"].now() + i - 1)
                    nk = it["nk"]
                    do(A_(probT[:, i % 2, 0:nk // P, :], o[:, 0:nk].rearrange("p (a n) -> p a n", n=P), ACT.Copy),
                       free, probT_ready)

                exps(0, items[0])
                for i, it in enumerate(items):
                    if i + 1 < len(items):
                        exps(i + 1, items[i + 1])
                    turned(i, it)
                    if i in spread_at:
                        small.up()
                tl["probn"].up(len(items))
                tl["pv"].up(len(items))

            def hybrid(l):
                def step_v(k=1):
                    act.wait_ge(v_hyb, tl["vh"].up(k))

                squares(CTX)
                root_wide([1])
                small.up()
                for k in range(DC):
                    act.wait_ge(n_ready, tl["n"].up())
                    A_(uR[:, 0, k, CTX:T], yT[:, k, CTX:T], ACT.Copy).then_inc(uh_ready, 1)
                step_v()
                for n in range(len(HY)):
                    if n in (3, 4, 5, 6, 7, 8, 11, 14):
                        gemm.up()
                        lead_next()
                        continue
                    o, free = product()
                    lead_next()
                    o3 = o[:, :].rearrange("p (a n) -> p a n", a=2)
                    if n == 0:
                        do(A_(cq, o3, ACT.Copy), free)
                    elif n == 1:
                        do(A_(ckv, o[:, 0:SEQ], ACT.Copy))
                        do(A_(mk[64:96, 0, :], o[64:96, SEQ:T], ACT.Copy), free)
                    elif n == 12:
                        do(A_(mbq, o3, ACT.Copy, scale=0.125), free)
                    elif n == 13:
                        do(A_(mbk, o3, ACT.Copy), free)
                    else:
                        dst = {2: mgate, 9: gz[:, 0:2, :], 10: gz[:, 2:4, :], 15: cgate}[n]
                        do(A_(dst, o3, ACT.Silu), free)
                do(A_(half[:, 0, :], cq, ACT.Square))
                do(A_(half[:, 1, 0:SEQ], ckv, ACT.Square), a_act)
                root(4)
                small.up(3)
                step_v()
                for g in range(3):
                    do(A_(cvo[:, 4 * g:4 * g + 4, :], cvo[:, 4 * g:4 * g + 4, :], ACT.Silu))
                do(A_(hsq, cvo[:, 0:8, :], ACT.Square))
                do(A_(gs[:, 6, :], gs[:, 4, :], ACT.Exp))
                do(A_(gs[:, 7, :].rearrange("p (a n) -> p a n", a=2), gs[:, 0:2, 0:GH], ACT.Exp, scale=-1.0))
                do(A_(gs[:, 8, 0:GH], galog[:, l, 0, :], ACT.Exp))
                do(A_(gs[:, 6, :], gs[:, 6, :], ACT.Ln, bias=1.0), a_act)
                step_v(2)
                for p in range(2):
                    o, free = product()
                    do(A_(mq[0:MLA_QK, 2 * p:2 * p + 2, :], o[0:MLA_QK, :].rearrange("p (a n) -> p a n", a=2), ACT.Copy,
                          scale=STEPS), free, a_act)
                for p in range(2):
                    o, free = product()
                    do(A_(mk[0:NOPE, 2 * p:2 * p + 2, :], o[0:NOPE, :].rearrange("p (a n) -> p a n", a=2), ACT.Copy),
                       free, a_act)
                gemm.up(2)
                small.up(4)
                root(16)
                step_v(5)
                attention([*mla_items(), *moba_items()], SPREAD_AT)
                step_v(1 + 4)
                for dst in (ktok, vtk):
                    for t in range(2):
                        o, free = product()
                        do(A_(dst[:, 4 * t:4 * t + 4, :], o[:, :].rearrange("p (a n) -> p a n", n=P), ACT.Copy), free)
                act.sem_inc(a_act, 1)
                small.up()
                step_v()
                gemm.up()
                o, free = product()
                do(A_(EG, o[:, :].rearrange("p (a n) -> p a n", n=P), ACT.Exp), free)
                do(A_(DTm, DTm, ACT.Exp))
                do(A_(gs[:, 11, 0:GH], gs[:, 11, 0:GH], ACT.Exp))
                do(A_(gs[:, 12, :], gs[:, 10, :], ACT.Exp), a_act)
                gemm.up(4)
                step_v()
                gemm.up(2)
                step_v()
                for t in range(2):
                    o, free = product()
                    do(A_(LT[:, 4 * t:4 * t + 4, :], o[:, :].rearrange("p (a n) -> p a n", n=P), ACT.Copy), free, a_act)
                for m in range(1, LEVELS):
                    for t in range(2):
                        o, free = product()
                        do(A_(Ym[:, 4 * t:4 * t + 4, :], o[:, :].rearrange("p (a n) -> p a n", n=P), ACT.Copy),
                           free, a_act)
                    gemm.up(2 if m == LEVELS - 1 else 4)
                step_v(1 + 3 * (LEVELS - 2) + 2)

                def keep(dst):
                    o, free = product()
                    do(A_(dst, o[:, :].rearrange("p (a n) -> p a n", n=P), ACT.Copy), free, a_act)

                keep(Um[:, 0:4, :])
                keep(S1)
                keep(oraw[:, :, 0:P])
                gemm.up()
                step_v()
                keep(Um[:, 4:8, :])
                o, free = product()
                do(A_(oraw[:, :, P:2 * P], o[:, :].rearrange("p (a n) -> p a n", n=P), ACT.Copy), free)
                do(A_(hsq[:, 0:4, :], oraw, ACT.Square), a_act)
                root(8)
                small.up(3)
                for k in (0, 6):
                    A_(uR[:, 0, k:k + 2, CTX:T], yc[:, k:k + 2, :], ACT.Copy).then_inc(uh_ready, 1)
                for k in (2, 4):
                    step_v()
                    A_(uR[:, 0, k:k + 2, CTX:T], yc[:, k:k + 2, :], ACT.Copy).then_inc(uh_ready, 1)
                for b in range(4):
                    gemm.up()
                    lead_next()

            tl["g"].up()
            act.wait_ge(vec_ready, 1)
            do(A_(sc[:, :, 0], vec[:, 0, V_CC:V_CC + DC], ACT.Silu))
            do(A_(sc[:, :, 1], vec[:, 0, V_C:V_C + DC], ACT.Silu), sc_ready)
            small.up(2)
            gemm.up(DC)
            act.wait_ge(lam_exp, 1)
            do(A_(lams[:, 2:4], lams[:, 0:2], ACT.Exp), lam_exp)
            act.sem_inc(ada_free, 2)
            for b in range(2):
                act.sem_inc(rows_out[b], 16)
            abank, out_rows = Banks(6, 2), Tally()
            for l in range(LAYERS):
                with repeat(act, 3, (abank, 6), (own, 6), (out_rows, 48)) as i:
                    for b in range(6):
                        bank_no, full, _ = abank.take()
                        act.wait_ge(ada_done, full)
                        if b % 2 == 0:
                            out_rows.up(16)
                        act.wait_ge(rows_out[b % 2], out_rows.now())
                        do(A_(half[0:2, b % 2, :], psum[bank_no][0:2, :], ACT.Copy), ada_free)
                        act.dma_start(rows_dram[l][:, bass.ds(i * 3072 + b * 512, 512)],
                                      half[0:2, b % 2, :]).then_inc(rows_out[b % 2], 16)
            small.up()
            for b in range(2):
                lead_next()

            for st in run:
                c0, streams = shape_of(st)
                if st in SUB:
                    l, sub = SUB[st]
                    squares(0 if st == "na" else c0)
                    root_wide([0, 1] if st == "na" else streams)
                    small.up()
                    shift(l, sub, [0, 1] if st == "na" else streams)
                if st.startswith("ffn"):
                    w = T - c0
                    one = "p (a n) -> p a n"
                    for part, kc in enumerate((F0, FC - F0)):
                        with repeat(act, kc // 2, (gemm, 4), (own, 6), (tl["g"], 2), (tl["gm"], 2), (tl["w0"], 32),
                                    (tl["w1"], 32), (tl["split"], 2)) as i:
                            for s in range(2):
                                o, _ = product()
                                act.wait_ge(g_ready, tl["g"].now())
                                tl["g"].up()
                                do(A_(half[:, s, 0:w], o[:, 0:w], ACT.Silu), silu_ready)
                                gemm.up()
                                lead(s)
                                act.wait_ge(gm_ready, tl["gm"].up())
                                do(A_(gR[:, 0, bass.ds(i * 2 + s, 1), c0:T], half[:, s:s + 1, 0:w], ACT.Copy), gh_ready)
                        if part == 0:
                            with repeat(act, 2, (gemm, 4), (own, 8), (tl["w0"], 64), (tl["w1"], 64),
                                        (tl["split"], 4)) as i:
                                for b in range(4):
                                    o, free = product()
                                    do(A_(yT[:, bass.ds(i * 4 + b, 1), c0:T], o[:, 0:w].rearrange(one, a=1), ACT.Copy),
                                       free)
                                    lead(b % 2)
                    warm_root()
                    for k in range(DC):
                        gemm.up()
                        act.wait_ge(y_added, tl["yadd"].up())
                        do(A_(sqT[:, k, c0:T], yT[:, k, c0:T], ACT.Square), sq_ready)
                        lead_next()
                    root((T - c0) // P)
                    small.up(2)
                elif st in ("da", "na"):
                    for which, q0 in enumerate((c0, 0)):
                        with repeat(act, 2, (gemm, 4), (own, 6), (tl["w0"], 32), (tl["w1"], 32), (tl["split"], 2)) as i:
                            for s in range(2):
                                for j in range(2):
                                    o, free = product()
                                    do(A_(bigc[:, bass.ds(i * 4 + (8 * which + 2 * s + j), 1), q0:T],
                                          o[:, 0:T - q0].rearrange("p (a n) -> p a n", a=1), ACT.Copy,
                                          scale=0.125 if st == "na" and which == 0 else 1.0), free, qkv_ready)
                                lead(s)
                    with repeat(act, 2, (gemm, 8), (own, 2), (tl["w0"], 32), (tl["w1"], 32), (tl["split"], 2)) as i:
                        for s in range(2):
                            gemm.up(4)
                            lead(s)
                    if st == "da":
                        small.up(16)
                    attention(da_items() if st == "da" else na_items())
                    if st == "da":
                        for h in range(8):
                            act.wait_ge(o_ready, h + 1)
                            do(A_(sqT[:, h, :], bigc[:, h, :], ACT.Square), sq_ready)
                        root(8 * TT)
                        small.up(9)
                    if st == "na":
                        warm_root()
                    split_heads(c0)
                    for k in range(DC):
                        o, free = product()
                        do(A_(yT[:, k, c0:T], o[:, 0:T - c0], ACT.Copy))
                        do(A_(bigc[:, DC + k, c0:T], o[:, 0:T - c0], ACT.Square), free, sq_ready)
                        if k % 2 == 1:
                            lead_next()
                    root((T - c0) // P)
                    small.up(2)
                elif st.startswith("hy"):
                    hybrid(int(st[2]))
            if stop is None:
                squares(CTX)
                root_wide([1])
                small.up()
                for t in range(2):
                    for g in range(2):
                        o, free = product()
                        do(A_(stage[:, t, g * 512:(g + 1) * 512], o[:, :], ACT.Copy), free)
            act.sem_inc(out_ready, 1)

        @block.vector
        def _(dve):
            gemm, small = Banks(0, 4), Banks(4, 2)
            own = Tally()
            tl = {k: Tally() for k in ("root", "silu", "exp", "pv", "aa", "sq", "split", "uh", "gh")}
            V = nc.vector

            def do(ins, *signals):
                ins.then_inc(vec_step, 1)
                dve.wait_ge(vec_step, own.up())
                for s in signals:
                    dve.sem_inc(s, 1)

            def product(pool=None):
                pool = pool or gemm
                b, full, _ = pool.take()
                dve.wait_ge(gemm_full if pool is gemm else small_full, full)
                return psum[b], (gemm_free if pool is gemm else small_free)[b - pool.first]

            def norm_stats(n, means):
                o, free = product(small)
                for a, b, inv, eps in means:
                    do(V.tensor_scalar(stat[:, 0, a:b], o[:, a:b], inv, eps, ALU.mult, ALU.add))
                dve.sem_inc(free, 1)
                dve.sem_inc(var_ready, 1)
                dve.wait_ge(root_ready, tl["root"].up())
                do(V.reciprocal(stat[:, 1, 0:n], stat[:, 0, 0:n]))

            def diagonal(a, nt):
                do(V.tensor_tensor(diag[:, 0:nt * P].rearrange("p (a n) -> p a n", n=P), rep(ident, nt),
                                   wide(stat[:, 1, a:a + nt], P), ALU.mult), diag_ready)

            def spread(a, nt):
                diagonal(a, nt)
                return product(small)

            def spreads(firsts, nt, use):
                for n, a in enumerate(firsts):
                    if n == 0:
                        diagonal(a, nt)
                    r, free = product(small)
                    if n + 1 < len(firsts):
                        diagonal(firsts[n + 1], nt)
                    use(n, r, free)

            def stt(out_, in0, scalar, in1, op0=ALU.mult, op1=ALU.mult):
                return V.scalar_tensor_tensor(out=out_, in0=in0, scalar=scalar, in1=in1, op0=op0, op1=op1)

            def stream_norm(c0, streams):
                o, free = product(small)
                for s in streams:
                    a = s * CTX
                    do(V.tensor_scalar(rstd[:, a:a + SEQ], o[:, a - c0:a - c0 + SEQ], 1.0 / D, EPS, ALU.mult, ALU.add),
                       var_ready)
                dve.sem_inc(free, 1)
                for s in streams:
                    dve.wait_ge(root_ready, tl["root"].up())
                    r = rstd[:, s * CTX:s * CTX + SEQ]
                    do(V.reciprocal(r, r))

            def prenorm(i6, c0, streams):
                stream_norm(c0, streams)
                l, sub = i6 // 3, i6 % 3
                parts = [(k, s) for k in range(DC) for s in streams]
                for n in range(len(parts) + 2):
                    if n < len(parts):
                        k, s = parts[n]
                        a = slice(s * CTX, s * CTX + SEQ)
                        stt(yT[:, k, a], hT[:, k, a], coefA[:, i6, k, s:s + 1], rstd[:, a]).then_inc(n_ready, 1)
                    if n >= 2:
                        k, s = parts[n - 2]
                        a = slice(s * CTX, s * CTX + SEQ)
                        dve.wait_ge(uh_ready, tl["uh"].up())
                        stt(uR[:, 1, k, a], yT[:, k, a], mod[:, l, 3 * sub * DC + k, s:s + 1],
                            uR[:, 0, k, a].bitcast(F32), ALU.add, ALU.subtract).then_inc(u_ready, 1)

            def rest(s, n=SLOT):
                dve.wait_ge(w_hi, tl["split"].up())
                do(V.tensor_tensor(wl[:, s, 0:n], wraw[:, s, 0:n], wh[:, s, 0:n].bitcast(F32), ALU.subtract), w_lo)

            def rest_next():
                b = tl["split"].n
                if b < len(SIZES):
                    rest(b % 2, SIZES[b])

            def residual(i6, c0, streams, chunks, squares):
                for k in range(DC):
                    chunks(k)
                    dve.wait_ge(sq_ready, tl["sq"].up())
                    if k == 0:
                        do(V.tensor_copy(sqsum[:, c0:T], squares[:, 0, c0:T]))
                    else:
                        do(V.tensor_tensor(sqsum[:, c0:T], sqsum[:, c0:T], squares[:, k, c0:T], ALU.add))
                    if k < DC - 1 and (squares is sqT or k % 2 == 1):
                        rest_next()
                dve.sem_inc(sum_ready, 1)
                nt = (T - c0) // P
                norm_stats(nt, [(0, nt, 1.0 / D, EPS)])
                diagonal(0, nt)
                rest_next()
                r, free = product(small)
                scaled = []
                for k in range(DC + 1):
                    if k < DC:
                        for s in streams:
                            a = slice(s * CTX, s * CTX + SEQ)
                            stt(yT[:, k, a], yT[:, k, a], coefG[:, i6, k, s:s + 1],
                                r[:, s * CTX - c0:s * CTX - c0 + SEQ]).then_inc(vec_step, 1)
                            scaled.append(own.up())
                    if k:
                        dve.wait_ge(vec_step, scaled[k * len(streams) - 1])
                        V.tensor_tensor(hT[:, k - 1, c0:T], hT[:, k - 1, c0:T], yT[:, k - 1, c0:T],
                                        ALU.add).then_inc(h_ready, 1)
                dve.sem_inc(free, 1)

            def split_heads(k, c0):
                dve.wait_ge(uh_ready, tl["uh"].up())
                V.tensor_tensor(uR[:, 1, k, c0:T], bigc[:, k, c0:T], uR[:, 0, k, c0:T].bitcast(F32),
                                ALU.subtract).then_inc(on_ready, 1)

            def attention(items, take, spread_at=(), use=None):
                items = list(items)

                def turns(i):
                    return small.n + i + sum(j < i for j in spread_at)

                def table(i, it):
                    h, t = it["na"]
                    if i >= 2:
                        dve.wait_ge(gemm_full, gemm.n)
                    m = maskb[:, t, :].rearrange("p (r n) -> p r n", r=ROWS)
                    raw = rawb[t][h // HH][:, h % HH, 0:1]
                    raw = bass.AP(tensor=raw.tensor, offset=raw.offset, ap=[raw.ap[0], [RPB_C, ROWS], [1, GRID_W]])
                    do(V.tensor_tensor(m, raw, rep(c("win"), ROWS), ALU.mult))
                    do(V.tensor_tensor(m, m, rep(c("notwin"), ROWS), ALU.add), bias_ready)

                def peak(i, it):
                    for j in range(len(it["q"])):
                        o, _ = product()
                        do(V.reduce_max(negm[:, i % 2, 0, j:j + 1], o[:, 0:it["nk"]], AX.X))
                    n = len(it["q"])
                    do(V.tensor_scalar(negm[:, i % 2, 1, 0:n], negm[:, i % 2, 0, 0:n], -it["scale"], None, ALU.mult),
                       negm_ready)

                def normalise(i, it):
                    n, nk, b = len(it["q"]), it["nk"], i % 2
                    dve.wait_ge(exp_ready, tl["exp"].up())
                    do(V.reciprocal(rsum[:, b, 1, 0:n], rsum[:, b, 0, 0:n]))
                    if i >= 2:
                        dve.wait_ge(small_full, turns(i - 2) + 1)
                    if n == 2:
                        do(V.tensor_scalar(lams[:, 5:6], rsum[:, b, 1, 1:2], lams[:, 4:5], None, ALU.mult))
                        do(V.tensor_scalar(prob[:, b, 1, 0:nk], prob[:, b, 1, 0:nk], lams[:, 5:6], None, ALU.mult))
                        do(stt(probn[:, b, 0:nk], prob[:, b, 0, 0:nk], rsum[:, b, 1, 0:1], prob[:, b, 1, 0:nk],
                               ALU.mult, ALU.add), probn_ready)
                    else:
                        do(V.tensor_scalar(probn[:, b, 0:nk], prob[:, b, 0, 0:nk], rsum[:, b, 1, 0:1], None, ALU.mult),
                           probn_ready)

                def output(i):
                    if i % 4 == 3:
                        dve.wait_ge(pv_done, tl["pv"].now() + i + 1)
                        take(i // 4, psum[6 + obank[0] % 2])
                        obank[0] += 1

                if "na" in items[0]:
                    table(0, items[0])
                    table(1, items[1])
                peak(0, items[0])
                for i, it in enumerate(items):
                    if i + 2 < len(items) and "na" in it:
                        table(i + 2, items[i + 2])
                    if i + 1 < len(items):
                        peak(i + 1, items[i + 1])
                    normalise(i, it)
                    if i:
                        output(i - 1)
                    if i + 1 in spread_at:
                        diagonal(4 * spread_at.index(i + 1), 4)
                    if i - 1 in spread_at:
                        n = turns(i - 1) + 1
                        dve.wait_ge(small_full, n + 1)
                        use(spread_at.index(i - 1), psum[small.first + n % 2], small_free[n % 2])
                output(len(items) - 1)
                small.up(len(items) + len(spread_at))
                tl["pv"].up(len(items))

            obank = [0]

            def hybrid(l):
                def step_a(k=1):
                    dve.wait_ge(a_act, tl["aa"].up(k))

                stream_norm(CTX, [1])
                for n in range(DC + 1):
                    if n < DC:
                        stt(yT[:, n, CTX:T], hT[:, n, CTX:T], vec[:, 0, V_NW + l * DC + n:V_NW + l * DC + n + 1],
                            rstd[:, CTX:T]).then_inc(n_ready, 1)
                    if n:
                        dve.wait_ge(uh_ready, tl["uh"].up())
                        V.tensor_tensor(uR[:, 1, n - 1, CTX:T], yT[:, n - 1, CTX:T],
                                        uR[:, 0, n - 1, CTX:T].bitcast(F32), ALU.subtract).then_inc(u_ready, 1)
                tl["sq"].up(DC)
                dve.sem_inc(v_hyb, 1)
                do(V.memset(convin[:, :, 0:PAD], 0.0))

                def convolve(k):
                    for j in range(CONV):
                        w = vec[:, 3, (l * CONV + j) * 12 + k:(l * CONV + j) * 12 + k + 1]
                        x = convin[:, k, j:j + SEQ]
                        if j == 0:
                            do(V.tensor_scalar(cvo[:, k, :], x, w, None, ALU.mult))
                        else:
                            do(stt(cvo[:, k, :], x, w, cvo[:, k, :], ALU.mult, ALU.add))

                for n in range(len(HY)):
                    if 3 <= n <= 8:
                        o, free = product()
                        do(V.tensor_copy(convin[:, 2 * (n - 3):2 * (n - 3) + 2, PAD:PAD + SEQ],
                                         o[:, :].rearrange("p (a n) -> p a n", a=2)), free)
                    elif n == 11:
                        o, free = product()
                        do(V.tensor_copy(gs[:, 0:2, :], o[:, 0:16].rearrange("p (a n) -> p a n", a=2)), free)
                    elif n == 14:
                        o, free = product()
                        do(V.tensor_copy(mbv, o[:, :].rearrange("p (a n) -> p a n", a=2)), free)
                    else:
                        gemm.up()
                    rest_next()
                    if n >= 4:
                        convolve(n - 4)
                ab = gs[:, 0:2, GH:2 * GH]

                def g2(j):
                    return gs[:, j, :].rearrange("p (a n) -> p a n", a=2)

                do(V.tensor_tensor(g2(3), ab, rep(galog[:, l, 1, :], 2), ALU.add))
                do(V.tensor_scalar(gs[:, 4, :], gs[:, 3, :], -1.0, None, ALU.mult))
                do(V.tensor_scalar(gs[:, 5, :], gs[:, 3, :], 0.0, None, ALU.max))
                do(V.tensor_tensor(gs[:, 4, :], gs[:, 3, :], gs[:, 4, :], ALU.min), v_hyb)
                step_a()
                norm_stats(4, [(0, 2, 1.0 / 256, EPS), (2, 4, 1.0 / 128, EPS)])
                r, free = spread(0, 2)
                for k in range(2):
                    do(stt(cq[:, k, :], cq[:, k, :], vec[:, 1, V_Q + 2 * l + k:V_Q + 2 * l + k + 1], r[:, 0:SEQ]))
                dve.sem_inc(free, 1)
                dve.sem_inc(v_hyb, 1)
                r, free = spread(2, 2)
                do(stt(ckv, ckv, vec[:, 1, V_KV + l:V_KV + l + 1], r[:, 0:SEQ]), free, v_hyb)
                step_a(5)
                gemm.up(4)
                for t in range(2):
                    o, free = product()
                    do(V.tensor_copy(mv[:, t, :].rearrange("p (h n) -> p h n", h=4),
                                     o[:, :].rearrange("p (h n) -> p h n", h=4)[:, :, NOPE:P]), free, v_hyb)
                for p in range(2):
                    o, free = product(small)
                    x = mq[0:MLA_QK, 2 * p:2 * p + 2, :]
                    tmp = half[0:MLA_QK, 0, :].rearrange("p (a n) -> p a n", a=2)
                    do(V.tensor_tensor(tmp, o[0:MLA_QK, :].rearrange("p (a n) -> p a n", a=2),
                                       rep(c("sin96")[0:MLA_QK, :], 2), ALU.mult), free)
                    do(V.tensor_tensor(x, x, rep(c("cos96")[0:MLA_QK, :], 2), ALU.mult))
                    do(V.tensor_tensor(x, x, tmp, ALU.add), v_hyb)
                o, free = product(small)
                do(V.tensor_tensor(half[64:96, 0, 0:SEQ], o[64:96, 0:SEQ], c("sin96")[64:96, :], ALU.mult), free)
                do(V.tensor_tensor(half[64:96, 1, 0:SEQ], mk[64:96, 0, :], c("cos96")[64:96, :], ALU.mult))
                do(V.tensor_tensor(mk[64:96, :, :], rep(half[64:96, 0, 0:SEQ], 4), rep(half[64:96, 1, 0:SEQ], 4),
                                   ALU.add), v_hyb)
                norm_stats(16, [(0, 16, 1.0, EPS)])
                do(V.tensor_tensor(gs[:, 5, :], gs[:, 5, :], gs[:, 6, :], ALU.add))
                do(stt(g2(9), g2(5), -1.0, rep(gs[:, 8, 0:GH], 2)))
                do(V.tensor_scalar(gs[:, 7, :], gs[:, 7, :], 1.0, None, ALU.add))
                do(V.reciprocal(gs[:, 2, :], gs[:, 7, :]))
                do(V.tensor_copy(gB, wide(gs[:, 9, :], P)), v_hyb)

                def take(k, o):
                    gate = (mgate if k < 2 else cgate)[:, k % 2, :]
                    do(V.tensor_tensor(yc[:, (0, 1, 6, 7)[k], :], o[:, 0:SEQ], gate, ALU.mult), o_taken)

                def scale_qk(p, r, free):
                    x = cvo[:, 2 * p:2 * p + 2, :]
                    do(stt(x, x, P ** -0.5 if p < 2 else 1.0, r[:, :].rearrange("p (a n) -> p a n", a=2)), free, v_hyb)

                attention([*mla_items(), *moba_items()], take, SPREAD_AT, scale_qk)

                gemm.up(4)
                o, free = product(small)
                do(V.tensor_copy(gs[:, 10, :], o[:, 0:GN]), free)
                for t in range(2):
                    o, free = product()
                    for h in range(GH):
                        n = 4 * t + h
                        do(stt(DTm[:, n, :], o[:, h * P:h * P + P], gs[:, 10, n:n + 1], c("future"), ALU.subtract,
                               ALU.add))
                    if t == 0:
                        do(V.tensor_tensor(gs[:, 11, 0:GH], o[:, :].rearrange("p (a n) -> p a n", n=P)[:, :, P - 1],
                                           gs[:, 10, 0:GH], ALU.subtract), free)
                dve.sem_inc(v_hyb, 1)
                step_a(2)
                do(stt(gs[:, 13, :], gs[:, 2, :], -1.0, gs[:, 12, :]))
                do(V.tensor_tensor(qg, EG, cvo[:, 0:GH, P:2 * P], ALU.mult))
                do(V.tensor_tensor(ktok[:, 0:GH, :], ktok[:, 0:GH, :], wide(gs[:, 11, 0:GH], P), ALU.mult))
                do(V.tensor_tensor(vtk, vtk, wide(gs[:, 2, :], P), ALU.mult))
                for t in range(2):
                    o, free = product()
                    x = LT[:, 4 * t:4 * t + 4, :]
                    do(V.tensor_tensor(x, o[:, :].rearrange("p (a n) -> p a n", n=P), DTm[:, 4 * t:4 * t + 4, :],
                                       ALU.mult), free)
                    do(V.tensor_tensor(x, x, rep(c("strict"), 4), ALU.mult))
                dve.sem_inc(v_hyb, 1)
                for t in range(2):
                    o, free = product()
                    do(V.tensor_tensor(ATm[:, 4 * t:4 * t + 4, :], o[:, :].rearrange("p (a n) -> p a n", n=P),
                                       DTm[:, 4 * t:4 * t + 4, :], ALU.mult), free)
                for t in range(2):
                    o, free = product()
                    do(V.tensor_tensor(Ym[:, 4 * t:4 * t + 4, :], o[:, :].rearrange("p (a n) -> p a n", n=P),
                                       wide(gs[:, 2, 4 * t:4 * t + 4], P), ALU.mult), free)
                dve.sem_inc(v_hyb, 1)
                do(V.tensor_tensor(Xm, Ym, rep(c("low0"), GN), ALU.mult))
                do(stt(Xm, Xm, -1.0, rep(ident, GN), ALU.mult, ALU.add))
                gemm.up(2)
                step_a(2)

                def level(m):
                    a = CONST_COLS["lowT"][0] + m * P
                    return rep(cst[:, a:a + P], GN)

                do(V.tensor_tensor(XT, LT, level(0), ALU.mult))
                do(stt(XT, XT, -1.0, rep(ident, GN), ALU.mult, ALU.add))
                do(V.tensor_tensor(LmT, LT, level(1), ALU.mult), v_hyb)
                for m in range(1, LEVELS):
                    gemm.up(2)
                    step_a(2)
                    if m < LEVELS - 1:
                        do(V.tensor_tensor(LmT, LT, level(m + 1), ALU.mult), v_hyb)
                    for t in range(2):
                        for which in range(2):
                            if which == 0 and m == LEVELS - 1:
                                continue
                            o, free = product()
                            x = (XT if which else Xm)[:, 4 * t:4 * t + 4, :]
                            do(V.tensor_tensor(x, x, o[:, :].rearrange("p (a n) -> p a n", n=P), ALU.subtract), free)
                        dve.sem_inc(v_hyb, 1)
                gemm.up(3)
                step_a(3)
                o, free = product()
                x = Rm[:, 4:8, :]
                do(V.tensor_tensor(x, o[:, :].rearrange("p (a n) -> p a n", n=P), wide(gs[:, 13, 4:8], P), ALU.mult),
                   free)
                do(V.tensor_tensor(x, x, vtk[:, 4:8, :], ALU.add), v_hyb)
                gemm.up(2)
                step_a(2)
                norm_stats(8, [(0, 8, 1.0 / P, EPS)])

                def rest_of(k):
                    dve.wait_ge(uh_ready, tl["uh"].up())
                    V.tensor_tensor(uR[:, 1, k:k + 2, CTX:T], yc[:, k:k + 2, :],
                                    uR[:, 0, k:k + 2, CTX:T].bitcast(F32), ALU.subtract).then_inc(u_ready, 1)


                def scale_out(p, r, free):
                    x = oraw[:, 2 * p:2 * p + 2, :]
                    do(stt(x, x, vec[:, 1, V_GN + l:V_GN + l + 1], r[:, :].rearrange("p (a n) -> p a n", a=2)), free)
                    do(V.tensor_tensor(yc[:, 2 + 2 * p:4 + 2 * p, :], x, gz[:, 2 * p:2 * p + 2, :], ALU.mult), v_hyb)

                spreads([0, 4], 4, scale_out)
                for k in (0, 6, 2, 4):
                    rest_of(k)
                for b in range(4):
                    o, free = product()
                    x = hT[:, 2 * b:2 * b + 2, CTX:T]
                    do(V.tensor_tensor(x, x, o[:, :].rearrange("p (a n) -> p a n", a=2), ALU.add), free, h_ready,
                       h_ready)
                    rest_next()

            dve.sem_inc(g_ready, 2)
            do(V.memset(t5w[0:32, 4:5], 0.0))
            do(V.memset(t5w[32:33, :], 1.0), t5_set)
            o, free = product(small)
            for j, r in enumerate((128, 89, 72, 96)):
                do(V.tensor_copy(vec[:, j, 0:r], o[:, j * P:j * P + r]))
            dve.sem_inc(free, 1)
            dve.sem_inc(vec_ready, 1)
            for k in range(DC):
                o, free = product()
                do(V.tensor_copy(hT[:, k, :], o[:, :]), free, h_ready)
            o, free = product(small)
            do(V.tensor_copy(tline, o[0:5, 0:TAB]), free, line_ready)
            dve.wait_ge(lam_in, 16)
            for j in range(2):
                do(V.tensor_tensor_reduce(half[:, 0, 0:64], lamv[:, 128 * j:128 * j + 64],
                                          lamv[:, 128 * j + 64:128 * j + 128], 1.0, 0.0, ALU.mult, ALU.add,
                                          lams[:, j:j + 1]))
            dve.sem_inc(lam_exp, 1)
            dve.wait_ge(lam_exp, 2)
            do(V.tensor_tensor(lams[:, 4:5], lams[:, 3:4], lams[:, 2:3], ALU.subtract))
            do(V.tensor_scalar(lams[:, 4:5], lams[:, 4:5], -LAM_INIT, None, ALU.add))
            do(V.tensor_scalar(lams[:, 6:7], vec[:, 1, V_SUB:V_SUB + 1], 1.0 - LAM_INIT, None, ALU.mult))
            o, free = product(small)
            for l in range(LAYERS):
                a = 2 * l * N_MOD * DC
                do(V.tensor_tensor(mod[:, l], o[:, a:a + 2 * N_MOD * DC].rearrange("p (s c) -> p c s", s=2),
                                   wide(vec[:, 1 + l, 0:N_MOD * DC], 2), ALU.add), *([free] if l == LAYERS - 1 else []))
                for sub in range(3):
                    i6 = 3 * l + sub
                    m = mod[:, l]
                    do(stt(coefA[:, i6], m[:, (3 * sub + 1) * DC:(3 * sub + 2) * DC, :], 1.0, wide(v_norm(l, 2 * sub), 2),
                           ALU.add, ALU.mult))
                    do(stt(coefG[:, i6], m[:, (3 * sub + 2) * DC:(3 * sub + 3) * DC, :], 1.0 if sub == 1 else 0.5,
                           wide(v_norm(l, 2 * sub + 1), 2)))
            for b in range(2):
                rest_next()

            for st in run:
                c0, streams = shape_of(st)
                if st in SUB:
                    l, sub = SUB[st]
                    both = st == "na"
                    prenorm(3 * l + sub, 0 if both else c0, [0, 1] if both else streams)
                    tl["sq"].up(DC)
                if st.startswith("ffn"):
                    w = T - c0
                    for part, kc in enumerate((F0, FC - F0)):
                        with repeat(dve, kc // 2, (gemm, 4), (own, 6), (tl["silu"], 2), (tl["gh"], 2),
                                    (tl["split"], 2)) as i:
                            for s in range(2):
                                _, free_a = product()
                                o, free_b = product()
                                dve.wait_ge(silu_ready, tl["silu"].up())
                                do(V.tensor_tensor(half[:, s, 0:w], half[:, s, 0:w], o[:, 0:w], ALU.mult),
                                   free_a, free_b, gm_ready)
                                rest(s)
                                dve.wait_ge(gh_ready, tl["gh"].up())
                                k = bass.ds(i * 2 + s, 1)
                                do(V.tensor_tensor(gR[:, 1, k, c0:T], half[:, s:s + 1, 0:w],
                                                   gR[:, 0, k, c0:T].bitcast(F32), ALU.subtract), g_ready)
                        if part == 0:
                            with repeat(dve, 2, (gemm, 4), (own, 4), (tl["split"], 4)) as i:
                                for b in range(4):
                                    gemm.up()
                                    rest(b % 2)

                    def add(k):
                        o, free = product()
                        do(V.tensor_tensor(yT[:, k, c0:T], yT[:, k, c0:T], o[:, 0:w], ALU.add), free, y_added)

                    residual(3 * l + sub, c0, streams, add, sqT)
                elif st in ("da", "na"):
                    for turn in range(2):
                        with repeat(dve, 2, (gemm, 4), (own, 2), (tl["split"], 2)) as i:
                            for s in range(2):
                                gemm.up(2)
                                rest(s)
                    more = [(small, 8)] if st == "da" else []
                    with repeat(dve, 2, (gemm, 8), (own, 10 + (24 if st == "da" else 0)), (tl["split"], 2), *more) as i:
                        for s in range(2):
                            for t in range(TT):
                                o, free = product()
                                do(V.tensor_copy(vtok[:, t, bass.ds(i * 512 + s * 256, 256)], o[:, 0:256]), free, v_ready)
                                if st == "da":
                                    o, free = product(small)
                                    x = bigc[:, bass.ds(i * 8 + s * 4 + t, 1), CTX:T]
                                    one = "p (a n) -> p a n"
                                    do(V.tensor_tensor(half[:, 0, 0:SEQ], o[:, 0:SEQ], c("sin"), ALU.mult), free)
                                    do(V.tensor_tensor(x, x, c("cos").rearrange(one, a=1), ALU.mult))
                                    do(V.tensor_tensor(x, x, half[:, 0, 0:SEQ].rearrange(one, a=1), ALU.add), rope_ready)
                            rest(s)
                    if st == "da":
                        def take(k, o):
                            do(V.tensor_copy(bigc[:, k, :], o[:, :]), o_taken, o_ready)
                    else:
                        dve.wait_ge(rawb_in, 16 * 8)

                        def take(k, o):
                            do(V.tensor_copy(bigc[:, k, CTX:T], o[:, 0:SEQ]), o_taken, head_ready)
                    attention(da_items() if st == "da" else na_items(), take)
                    if st == "da":
                        tl["sq"].up(8)
                        norm_stats(32, [(0, 32, 1.0 / P, EPS)])

                        def scale_head(h, r, free):
                            do(stt(bigc[:, h, :], bigc[:, h, :], lams[:, 6:7], r[:, :]), free, head_ready)
                            if h:
                                split_heads(h - 1, c0)

                        spreads([4 * h for h in range(8)], 4, scale_head)
                        split_heads(7, c0)
                    else:
                        for h in range(8):
                            split_heads(h, c0)
                    residual(3 * l + sub, c0, streams, lambda k: gemm.up(), bigc[:, DC:2 * DC, :])
                elif st.startswith("hy"):
                    hybrid(int(st[2]))
            if stop is None:
                stream_norm(CTX, [1])
                for k in range(DC):
                    do(stt(bigc[:, k, CTX:T], hT[:, k, CTX:T], vec[:, 1, V_FIN + k:V_FIN + k + 1], rstd[:, CTX:T]))
                dve.sem_inc(v_hyb, 1)
            else:
                dve.sem_inc(out_ready, 1)



INS = ["x", "c", "ctx", "c_ctx", "ada_w", "ada_b", "norm_g", "ffn_w_in", "ffn_w_out", "da_w_in", "da_w_out",
       "da_lambda", "da_subln_g", "na_w_in", "na_w_out", "na_rpb", "norm_w_2", "w_in_2", "mla_q_norm_2",
       "mla_w_uq_2", "mla_kv_norm_2", "mla_w_ukv_2", "gdn_conv_w_2", "gdn_A_log_2", "gdn_dt_bias_2",
       "gdn_norm_w_2", "w_out_2", "t5_table_2", "final_norm_w_2"]


def kernel(**inputs):
    import concourse.bacc as bacc
    from concourse.bass_utils import run_bass_kernel_spmd

    nc = bacc.Bacc("TRN2", target_bir_lowering=False, num_devices=1)
    arrays, A = {}, {}
    for name in INS:
        a = np.ascontiguousarray(inputs[name])
        arrays[f"in_{name}"] = a
        A[name] = nc.dram_tensor(f"in_{name}", a.shape, F32, kind="ExternalInput").ap()
    arrays["in_constants"] = CONSTS
    const = nc.dram_tensor("in_constants", CONSTS.shape, F32, kind="ExternalInput").ap()
    tab = nc.dram_tensor("distance_lines", (5, TAB), F32).ap()
    out = nc.dram_tensor("out_rows", (1, SEQ, D), F32, kind="ExternalOutput").ap()
    rows = nc.dram_tensor("adaln_rows", (LAYERS, 2, N_MOD * D), F32).ap()
    build(nc, A, out, const, tab, rows)
    r = run_bass_kernel_spmd(nc, [arrays], core_ids=[0])
    return r.results[0]["out_rows"]
```
